# Optimizing a Trainium2 kernel written in Bass

```python
import math
import jax, jax.numpy as jnp
from jax import lax
import numpy as np

D_MODEL = 1024
BATCH = 1
SEQ = 512
DEPTH = 2

N_A_LAYERS = DEPTH // 2
N_B_LAYERS = DEPTH - N_A_LAYERS
RET_HEADS = 4
RET_QK_DIM = D_MODEL // RET_HEADS
RET_V_DIM = 2 * RET_QK_DIM
RET_CHUNK = 128
DIFF_HEAD_DIM = 64
DIFF_HEADS = D_MODEL // (2 * DIFF_HEAD_DIM)
Q_BLOCK = 128
D_FF = ((8 * D_MODEL // 3 + 127) // 128) * 128
CONV_WIDTH = 3
ROPE_BASE = 10000.0
EPS = 1e-6


def rms_norm(x, g=None):
    xf = x.astype(jnp.float32)
    y = xf * lax.rsqrt(jnp.mean(xf * xf, axis=-1, keepdims=True) + EPS)
    if g is not None:
        y = y * g.astype(jnp.float32)
    return y.astype(x.dtype)

def rotary(x, pos):
    half = x.shape[-1] // 2
    inv = 1.0 / (ROPE_BASE ** jnp.linspace(0.0, 1.0, half, dtype=jnp.float32))
    ang = pos.astype(jnp.float32)[:, None] * inv[None, :]
    cos = jnp.cos(ang)[None, :, None, :]
    sin = jnp.sin(ang)[None, :, None, :]
    xf = x.astype(jnp.float32)
    x1, x2 = xf[..., :half], xf[..., half:]
    return jnp.concatenate([x1 * cos - x2 * sin, x1 * sin + x2 * cos], axis=-1).astype(x.dtype)

def retention(xn, w_in, w_out):
    B, S, _ = xn.shape
    H, dk, dv, C = RET_HEADS, RET_QK_DIM, RET_V_DIM, RET_CHUNK
    dt = xn.dtype
    proj = xn @ w_in
    q, k, v, g = jnp.split(proj, [H * dk, 2 * H * dk, 2 * H * dk + H * dv], axis=-1)
    pos = jnp.arange(S)
    q = rotary(q.reshape(B, S, H, dk), pos)
    k = rotary(k.reshape(B, S, H, dk), pos) * (dk ** -0.5)
    v = v.reshape(B, S, H, dv)

    log_gamma = jnp.log1p(-jnp.power(2.0, -5.0 - jnp.arange(H, dtype=jnp.float32)))
    idx = jnp.arange(C, dtype=jnp.float32)
    rel = idx[:, None] - idx[None, :]
    decay_mask = jnp.where(rel[None] >= 0,
                           jnp.exp(log_gamma[:, None, None] * jnp.maximum(rel, 0.0)[None]),
                           0.0).astype(dt)
    q_decay = jnp.exp(log_gamma[None, :] * (idx[:, None] + 1.0)).astype(dt)
    k_decay = jnp.exp(log_gamma[None, :] * (C - 1.0 - idx[:, None])).astype(dt)
    chunk_decay = jnp.exp(log_gamma * C).astype(dt)

    n = S // C

    def to_chunks(t):
        return jnp.moveaxis(t.reshape(B, n, C, H, t.shape[-1]), 1, 0)

    def step(state, qkv):
        qc, kc, vc = qkv
        s = jnp.einsum('bihd,bjhd->bhij', qc, kc) * decay_mask[None]
        inner = jnp.einsum('bhij,bjhe->bihe', s, vc)
        cross = jnp.einsum('bihd,bhde->bihe', qc * q_decay[None, :, :, None], state)
        new_state = (state * chunk_decay[None, :, None, None]
                     + jnp.einsum('bjhd,bjhe->bhde', kc * k_decay[None, :, :, None], vc))
        return new_state, inner + cross

    state0 = jnp.zeros((B, H, dk, dv), dt)
    _, out = lax.scan(step, state0, (to_chunks(q), to_chunks(k), to_chunks(v)))
    out = jnp.moveaxis(out, 0, 1).reshape(B, S, H, dv)
    out = rms_norm(out).reshape(B, S, H * dv)
    return (jax.nn.silu(g) * out) @ w_out

def diff_attention(xn, k_sh, v_sh, w_q, lam_params, subln_g, w_out, lambda_init):
    B, S, _ = xn.shape
    H, d = DIFF_HEADS, DIFF_HEAD_DIM
    q = (xn @ w_q).reshape(B, S, H, 2, d) * (d ** -0.5)
    nb = S // Q_BLOCK
    q_blocks = jnp.moveaxis(q.reshape(B, nb, Q_BLOCK, H, 2, d), 1, 0)
    lp = lam_params.astype(jnp.float32)
    lam = jnp.exp(jnp.sum(lp[0] * lp[1])) - jnp.exp(jnp.sum(lp[2] * lp[3])) + lambda_init
    kpos = jnp.arange(S)

    def block(args):
        i, qb = args
        qpos = i * Q_BLOCK + jnp.arange(Q_BLOCK)
        s = jnp.einsum('bqhcd,bkhcd->bhcqk', qb, k_sh).astype(jnp.float32)
        s = jnp.where(kpos[None, :] <= qpos[:, None], s, -jnp.inf)
        p = jax.nn.softmax(s, axis=-1)
        a = p[:, :, 0] - lam * p[:, :, 1]
        return jnp.einsum('bhqk,bkhe->bqhe', a.astype(v_sh.dtype), v_sh)

    o = lax.map(block, (jnp.arange(nb), q_blocks))
    o = jnp.moveaxis(o, 0, 1).reshape(B, S, H, 2 * d)
    o = rms_norm(o, subln_g) * (1.0 - lambda_init)
    return o.reshape(B, S, H * 2 * d) @ w_out

def conv_ffn(xn, w_up, conv_w, conv_b, w_down):
    S = xn.shape[1]
    h = xn @ w_up
    hp = jnp.pad(h, ((0, 0), (CONV_WIDTH - 1, 0), (0, 0)))
    hc = conv_b
    for j in range(CONV_WIDTH):
        hc = hc + hp[:, j:j + S] * conv_w[j]
    g, u = jnp.split(hc, 2, axis=-1)
    return (jax.nn.silu(g) * u) @ w_down

def first_inputs(seed: int = 0) -> dict:
    key = jax.random.key(seed)
    ks = jax.random.split(key, 24)
    D, F = D_MODEL, D_FF
    ret_in = 2 * RET_HEADS * RET_QK_DIM + 2 * RET_HEADS * RET_V_DIM
    ret_v = RET_HEADS * RET_V_DIM
    diff_w = DIFF_HEADS * 2 * DIFF_HEAD_DIM

    def w(k, shape, fan_in):
        return jax.random.normal(k, shape, jnp.float32) * (fan_in ** -0.5)

    def gain(k, shape):
        return 1.0 + 0.02 * jax.random.normal(k, shape, jnp.float32)

    return {
        "x": jax.random.normal(ks[0], (BATCH, SEQ, D), jnp.float32),
        "a_norm_pre": gain(ks[1], (N_A_LAYERS, D)),
        "a_norm_post": gain(ks[2], (N_A_LAYERS, D)),
        "a_w_in": w(ks[3], (N_A_LAYERS, D, ret_in), D),
        "a_w_out": w(ks[4], (N_A_LAYERS, ret_v, D), ret_v),
        "kv_norm": gain(ks[5], (D,)),
        "w_kv": w(ks[6], (D, 2 * diff_w), D),
        "b_norm_pre": gain(ks[7], (N_B_LAYERS, D)),
        "b_norm_post": gain(ks[8], (N_B_LAYERS, D)),
        "b_w_q": w(ks[9], (N_B_LAYERS, D, diff_w), D),
        "b_lambda": 0.1 * jax.random.normal(ks[10], (N_B_LAYERS, 4, DIFF_HEAD_DIM), jnp.float32),
        "b_subln": gain(ks[11], (N_B_LAYERS, 2 * DIFF_HEAD_DIM)),
        "b_w_out": w(ks[12], (N_B_LAYERS, diff_w, D), diff_w),
        "ffn_norm_pre": gain(ks[13], (DEPTH, D)),
        "ffn_norm_post": gain(ks[14], (DEPTH, D)),
        "ffn_w_up": w(ks[15], (DEPTH, D, 2 * F), D),
        "ffn_conv_w": w(ks[16], (DEPTH, CONV_WIDTH, 2 * F), CONV_WIDTH),
        "ffn_conv_b": 0.02 * jax.random.normal(ks[17], (DEPTH, 2 * F), jnp.float32),
        "ffn_w_down": w(ks[18], (DEPTH, F, D), F),
    }

def first_block(x, a_norm_pre, a_norm_post, a_w_in, a_w_out, kv_norm, w_kv,
              b_norm_pre, b_norm_post, b_w_q, b_lambda, b_subln, b_w_out,
              ffn_norm_pre, ffn_norm_post, ffn_w_up, ffn_conv_w, ffn_conv_b, ffn_w_down):
    B, S, _ = x.shape
    H, d = DIFF_HEADS, DIFF_HEAD_DIM
    k_sh = None
    v_sh = None
    for layer in range(DEPTH):
        if layer < N_A_LAYERS:
            i = layer
            h = retention(rms_norm(x, a_norm_pre[i]), a_w_in[i], a_w_out[i])
            x = x + rms_norm(h, a_norm_post[i])
        else:
            i = layer - N_A_LAYERS
            if i == 0:
                kv = rms_norm(x, kv_norm) @ w_kv
                k_flat, v_flat = jnp.split(kv, 2, axis=-1)
                k_sh = k_flat.reshape(B, S, H, 2, d)
                v_sh = v_flat.reshape(B, S, H, 2 * d)
            lambda_init = 0.8 - 0.6 * math.exp(-0.3 * layer)
            h = diff_attention(rms_norm(x, b_norm_pre[i]), k_sh, v_sh, b_w_q[i],
                               b_lambda[i], b_subln[i], b_w_out[i], lambda_init)
            x = x + rms_norm(h, b_norm_post[i])
        h = conv_ffn(rms_norm(x, ffn_norm_pre[layer]), ffn_w_up[layer],
                     ffn_conv_w[layer], ffn_conv_b[layer], ffn_w_down[layer])
        x = x + rms_norm(h, ffn_norm_post[layer])
    return x


N_MIXERS = 2
N_CONV_LAYERS = (DEPTH + N_MIXERS - 1) // N_MIXERS
N_NSA_LAYERS = DEPTH // N_MIXERS
CONV_WIDTH_2 = 31
N_HEADS = 16
HEAD_DIM = 64
N_KV = 4
GROUP = N_HEADS // N_KV
ROT_DIM = HEAD_DIM // 4
ROPE_THETA = 500000.0
CMP_LEN = 32
CMP_STRIDE = 16
CMP_HIDDEN = 256
SEL_LEN = 64
SEL_TOPK = 16
WINDOW = 512
D_FF_2 = 2816
FFN_CONV_WIDTH = 3
PROJ_SIZES = (N_HEADS * HEAD_DIM,) + (N_KV * HEAD_DIM,) * 6 + (3 * N_HEADS,)
PROJ_COLS = sum(PROJ_SIZES)


def rmsnorm(x, g):
    xf = x.astype(jnp.float32)
    y = xf * lax.rsqrt(jnp.mean(xf * xf, axis=-1, keepdims=True) + EPS)
    return (y * g.astype(jnp.float32)).astype(x.dtype)

def layernorm(x, g, b):
    xf = x.astype(jnp.float32)
    mu = jnp.mean(xf, axis=-1, keepdims=True)
    var = jnp.mean(jnp.square(xf - mu), axis=-1, keepdims=True)
    y = (xf - mu) * lax.rsqrt(var + EPS)
    return (y * g.astype(jnp.float32) + b.astype(jnp.float32)).astype(x.dtype)

def causal_dwconv(x, w, b):
    width, ch = w.shape
    y = lax.conv_general_dilated(
        x, w[:, None, :].astype(x.dtype), window_strides=(1,),
        padding=[(width - 1, 0)], dimension_numbers=("NWC", "WIO", "NWC"),
        feature_group_count=ch)
    return y + b.astype(x.dtype)

def partial_rope(x):
    seq = x.shape[1]
    half = ROT_DIM // 2
    inv_freq = ROPE_THETA ** (-jnp.arange(half, dtype=jnp.float32) * (2.0 / ROT_DIM))
    ang = jnp.arange(seq, dtype=jnp.float32)[:, None] * inv_freq[None, :]
    cos = jnp.cos(ang)[:, None, :]
    sin = jnp.sin(ang)[:, None, :]
    xf = x.astype(jnp.float32)
    x1 = xf[..., :half]
    x2 = xf[..., half:ROT_DIM]
    out = jnp.concatenate([x1 * cos - x2 * sin, x2 * cos + x1 * sin, xf[..., ROT_DIM:]], axis=-1)
    return out.astype(x.dtype)

def masked_softmax(s, mask):
    s = jnp.where(mask, s.astype(jnp.float32), -1e30)
    m = jnp.max(s, axis=-1, keepdims=True)
    e = jnp.where(mask, jnp.exp(s - m), 0.0)
    return e / jnp.maximum(jnp.sum(e, axis=-1, keepdims=True), 1e-30)

def cmp_to_sel_matrix(n_cmp, n_sel):
    start_c = np.arange(n_cmp)[:, None] * CMP_STRIDE
    start_s = np.arange(n_sel)[None, :] * SEL_LEN
    ov = np.minimum(start_c + CMP_LEN, start_s + SEL_LEN) - np.maximum(start_c, start_s)
    return jnp.asarray(np.maximum(ov, 0).astype(np.float32) / CMP_LEN)

def conformer_conv(h, w_pw1, b_pw1, w_dw, b_dw, ln_g, ln_b, w_pw2, b_pw2):
    u = h @ w_pw1 + b_pw1
    a, gate = jnp.split(u, 2, axis=-1)
    u = a * jax.nn.sigmoid(gate)
    u = causal_dwconv(u, w_dw, b_dw)
    u = jax.nn.silu(layernorm(u, ln_g, ln_b))
    return u @ w_pw2 + b_pw2

def compress(blocks, pe, w1, w2):
    b, g, n, l, d = blocks.shape
    z = (blocks + pe).reshape(b, g, n, l * d)
    return jax.nn.silu(z @ w1) @ w2

def nsa_attention(h, w_in, q_g, kc_g, ks_g, kw_g, pe_k, pe_v, ck_w1, ck_w2, cv_w1, cv_w2, w_out):
    bsz, seq, _ = h.shape
    n_cmp = (seq - CMP_LEN) // CMP_STRIDE + 1
    n_sel = seq // SEL_LEN
    k_top = min(SEL_TOPK, n_sel)
    n_qb = seq // Q_BLOCK
    scale = HEAD_DIM ** -0.5

    splits = [int(c) for c in np.cumsum(PROJ_SIZES)[:-1]]
    q, kc, vc, ks, vs, kw, vw, gl = jnp.split(h @ w_in, splits, axis=-1)
    heads = lambda t, n: t.reshape(bsz, seq, n, HEAD_DIM)
    to_groups = lambda t: t.reshape(bsz, seq, N_KV, GROUP, HEAD_DIM).transpose(0, 2, 3, 1, 4)
    q = rmsnorm(heads(q, N_HEADS), q_g)
    q_nope = to_groups(q)
    q_rope = to_groups(partial_rope(q))
    gates = jax.nn.sigmoid(gl.astype(jnp.float32)).astype(h.dtype)
    gates = gates.reshape(bsz, seq, N_KV, GROUP, 3).transpose(0, 2, 3, 1, 4)

    blk_idx = np.arange(n_cmp)[:, None] * CMP_STRIDE + np.arange(CMP_LEN)[None, :]
    kc_blk = heads(kc, N_KV)[:, blk_idx].transpose(0, 3, 1, 2, 4)
    vc_blk = heads(vc, N_KV)[:, blk_idx].transpose(0, 3, 1, 2, 4)
    k_cmp = rmsnorm(compress(kc_blk, pe_k, ck_w1, ck_w2), kc_g)
    v_cmp = compress(vc_blk, pe_v, cv_w1, cv_w2)
    cmp_end = jnp.asarray(np.arange(n_cmp) * CMP_STRIDE + CMP_LEN - 1)
    cmp_map = cmp_to_sel_matrix(n_cmp, n_sel)

    k_sel = partial_rope(rmsnorm(heads(ks, N_KV), ks_g)).transpose(0, 2, 1, 3)
    k_sel = k_sel.reshape(bsz, N_KV, n_sel, SEL_LEN, HEAD_DIM)
    v_sel = heads(vs, N_KV).transpose(0, 2, 1, 3).reshape(bsz, N_KV, n_sel, SEL_LEN, HEAD_DIM)

    pad = ((0, 0), (0, 0), (WINDOW, 0), (0, 0))
    k_win = jnp.pad(partial_rope(rmsnorm(heads(kw, N_KV), kw_g)).transpose(0, 2, 1, 3), pad)
    v_win = jnp.pad(heads(vw, N_KV).transpose(0, 2, 1, 3), pad)

    b_ix = jnp.arange(bsz)[:, None, None, None]
    g_ix = jnp.arange(N_KV)[None, :, None, None]
    sel_off = jnp.arange(SEL_LEN)
    win_off = jnp.arange(Q_BLOCK + WINDOW)
    sel_ids = jnp.arange(n_sel)

    def query_block(qb):
        t0 = qb * Q_BLOCK
        pos = t0 + jnp.arange(Q_BLOCK)
        qn = lax.dynamic_slice_in_dim(q_nope, t0, Q_BLOCK, axis=3)
        qr = lax.dynamic_slice_in_dim(q_rope, t0, Q_BLOCK, axis=3)
        gt = lax.dynamic_slice_in_dim(gates, t0, Q_BLOCK, axis=3)

        s_c = jnp.einsum("bgrtd,bgnd->bgrtn", qn, k_cmp) * scale
        p_c = masked_softmax(s_c, cmp_end[None, :] <= pos[:, None])
        o_c = jnp.einsum("bgrtn,bgnd->bgrtd", p_c.astype(v_cmp.dtype), v_cmp)

        cur = pos // SEL_LEN
        imp = jnp.einsum("bgrtn,nj->bgtj", p_c, cmp_map)
        forced = (sel_ids[None, :] == 0) | (sel_ids[None, :] == cur[:, None]) | (sel_ids[None, :] == cur[:, None] - 1)
        imp = jnp.where(sel_ids[None, :] > cur[:, None], -1.0, jnp.where(forced, 1e4, imp))
        _, idx = lax.top_k(imp, k_top)
        k_g = k_sel[b_ix, g_ix, idx]
        v_g = v_sel[b_ix, g_ix, idx]
        s_s = jnp.einsum("bgrtd,bgtkld->bgrtkl", qr, k_g) * scale
        key_pos = idx[..., None] * SEL_LEN + sel_off
        mask_s = (key_pos <= pos[:, None, None]).reshape(bsz, N_KV, 1, Q_BLOCK, k_top * SEL_LEN)
        p_s = masked_softmax(s_s.reshape(bsz, N_KV, GROUP, Q_BLOCK, k_top * SEL_LEN), mask_s)
        o_s = jnp.einsum("bgrtm,bgtmd->bgrtd", p_s.astype(v_g.dtype),
                         v_g.reshape(bsz, N_KV, Q_BLOCK, k_top * SEL_LEN, HEAD_DIM))

        kwb = lax.dynamic_slice_in_dim(k_win, t0, Q_BLOCK + WINDOW, axis=2)
        vwb = lax.dynamic_slice_in_dim(v_win, t0, Q_BLOCK + WINDOW, axis=2)
        kp = t0 - WINDOW + win_off
        mask_w = (kp[None, :] >= 0) & (kp[None, :] <= pos[:, None]) & (kp[None, :] > pos[:, None] - WINDOW)
        s_w = jnp.einsum("bgrtd,bgsd->bgrts", qr, kwb) * scale
        p_w = masked_softmax(s_w, mask_w)
        o_w = jnp.einsum("bgrts,bgsd->bgrtd", p_w.astype(vwb.dtype), vwb)

        return gt[..., 0:1] * o_c + gt[..., 1:2] * o_s + gt[..., 2:3] * o_w

    o = lax.map(query_block, jnp.arange(n_qb))
    o = o.transpose(1, 0, 4, 2, 3, 5).reshape(bsz, seq, N_HEADS * HEAD_DIM)
    return o @ w_out

def conv_ffn_2(h, w_up, w_dw, b_dw, w_down):
    a, v = jnp.split(h @ w_up, 2, axis=-1)
    return (jax.nn.silu(causal_dwconv(a, w_dw, b_dw)) * v) @ w_down

def second_inputs(seed: int = 0) -> dict:
    key = jax.random.key(seed)
    ks = iter(jax.random.split(key, 40))
    f32 = jnp.float32
    D = D_MODEL
    hd = HEAD_DIM
    Lc = N_CONV_LAYERS
    Ln = N_NSA_LAYERS

    def w(shape, fan_in):
        return jax.random.normal(next(ks), shape, f32) * fan_in ** -0.5

    def gain(shape):
        return 1.0 + 0.05 * jax.random.normal(next(ks), shape, f32)

    def small(shape, s=0.02):
        return s * jax.random.normal(next(ks), shape, f32)

    return {
        "x": jax.random.normal(next(ks), (BATCH, SEQ, D), f32),
        "mix_norm_g": gain((DEPTH, D)),
        "ffn_norm_g": gain((DEPTH, D)),
        "conv_w_pw1": w((Lc, D, 2 * D), D),
        "conv_b_pw1": small((Lc, 2 * D)),
        "conv_w_dw": w((Lc, CONV_WIDTH_2, D), CONV_WIDTH_2),
        "conv_b_dw": small((Lc, D)),
        "conv_ln_g": gain((Lc, D)),
        "conv_ln_b": small((Lc, D)),
        "conv_w_pw2": w((Lc, D, D), D),
        "conv_b_pw2": small((Lc, D)),
        "nsa_w_in": w((Ln, D, PROJ_COLS), D),
        "nsa_q_norm": gain((Ln, hd)),
        "nsa_kc_norm": gain((Ln, hd)),
        "nsa_ks_norm": gain((Ln, hd)),
        "nsa_kw_norm": gain((Ln, hd)),
        "nsa_pe_k": small((Ln, CMP_LEN, hd), 0.1),
        "nsa_pe_v": small((Ln, CMP_LEN, hd), 0.1),
        "nsa_ck_w1": w((Ln, CMP_LEN * hd, CMP_HIDDEN), CMP_LEN * hd),
        "nsa_ck_w2": w((Ln, CMP_HIDDEN, hd), CMP_HIDDEN),
        "nsa_cv_w1": w((Ln, CMP_LEN * hd, CMP_HIDDEN), CMP_LEN * hd),
        "nsa_cv_w2": w((Ln, CMP_HIDDEN, hd), CMP_HIDDEN),
        "nsa_w_out": w((Ln, N_HEADS * hd, D), N_HEADS * hd),
        "ffn_w_up": w((DEPTH, D, 2 * D_FF_2), D),
        "ffn_w_dw": w((DEPTH, FFN_CONV_WIDTH, D_FF_2), FFN_CONV_WIDTH),
        "ffn_b_dw": small((DEPTH, D_FF_2)),
        "ffn_w_down": w((DEPTH, D_FF_2, D), D_FF_2),
    }

def second_block(x, mix_norm_g, ffn_norm_g,
              conv_w_pw1, conv_b_pw1, conv_w_dw, conv_b_dw, conv_ln_g, conv_ln_b, conv_w_pw2, conv_b_pw2,
              nsa_w_in, nsa_q_norm, nsa_kc_norm, nsa_ks_norm, nsa_kw_norm, nsa_pe_k, nsa_pe_v,
              nsa_ck_w1, nsa_ck_w2, nsa_cv_w1, nsa_cv_w2, nsa_w_out,
              ffn_w_up, ffn_w_dw, ffn_b_dw, ffn_w_down):
    for i in range(DEPTH):
        h = rmsnorm(x, mix_norm_g[i])
        j = i // N_MIXERS
        if i % N_MIXERS == 0:
            x = x + conformer_conv(h, conv_w_pw1[j], conv_b_pw1[j], conv_w_dw[j], conv_b_dw[j],
                                   conv_ln_g[j], conv_ln_b[j], conv_w_pw2[j], conv_b_pw2[j])
        else:
            x = x + nsa_attention(h, nsa_w_in[j], nsa_q_norm[j], nsa_kc_norm[j], nsa_ks_norm[j], nsa_kw_norm[j],
                                  nsa_pe_k[j], nsa_pe_v[j], nsa_ck_w1[j], nsa_ck_w2[j], nsa_cv_w1[j], nsa_cv_w2[j],
                                  nsa_w_out[j])
        x = x + conv_ffn_2(rmsnorm(x, ffn_norm_g[i]), ffn_w_up[i], ffn_w_dw[i], ffn_b_dw[i], ffn_w_down[i])
    return x


def setup_inputs(seed=0):
    out = dict(first_inputs(seed))
    for name, value in second_inputs(seed + 1).items():
        if name != "x":
            out[name + "_2"] = value
    return out


def reference(
    x, a_norm_pre, a_norm_post, a_w_in, a_w_out, kv_norm, w_kv, b_norm_pre, b_norm_post, b_w_q,
    b_lambda, b_subln, b_w_out, ffn_norm_pre, ffn_norm_post, ffn_w_up, ffn_conv_w, ffn_conv_b,
    ffn_w_down, mix_norm_g_2, ffn_norm_g_2, conv_w_pw1_2, conv_b_pw1_2, conv_w_dw_2,
    conv_b_dw_2, conv_ln_g_2, conv_ln_b_2, conv_w_pw2_2, conv_b_pw2_2, nsa_w_in_2, nsa_q_norm_2,
    nsa_kc_norm_2, nsa_ks_norm_2, nsa_kw_norm_2, nsa_pe_k_2, nsa_pe_v_2, nsa_ck_w1_2,
    nsa_ck_w2_2, nsa_cv_w1_2, nsa_cv_w2_2, nsa_w_out_2, ffn_w_up_2, ffn_w_dw_2, ffn_b_dw_2,
    ffn_w_down_2,
):
    x = first_block(
        x, a_norm_pre, a_norm_post, a_w_in, a_w_out, kv_norm, w_kv, b_norm_pre, b_norm_post,
        b_w_q, b_lambda, b_subln, b_w_out, ffn_norm_pre, ffn_norm_post, ffn_w_up, ffn_conv_w,
        ffn_conv_b, ffn_w_down,
    )
    return second_block(
        x, mix_norm_g_2, ffn_norm_g_2, conv_w_pw1_2, conv_b_pw1_2, conv_w_dw_2, conv_b_dw_2,
        conv_ln_g_2, conv_ln_b_2, conv_w_pw2_2, conv_b_pw2_2, nsa_w_in_2, nsa_q_norm_2,
        nsa_kc_norm_2, nsa_ks_norm_2, nsa_kw_norm_2, nsa_pe_k_2, nsa_pe_v_2, nsa_ck_w1_2,
        nsa_ck_w2_2, nsa_cv_w1_2, nsa_cv_w2_2, nsa_w_out_2, ffn_w_up_2, ffn_w_dw_2, ffn_b_dw_2,
        ffn_w_down_2,
    )


_drawn_inputs = setup_inputs


def setup_inputs(seed=0):
    import zlib

    import numpy as np

    out = dict(_drawn_inputs(seed))
    spreads = {}
    factors = {'kv_norm': 2.99,
     'b_norm_pre': 4.516,
     'b_norm_post': 5.005,
     'b_subln': 4.434,
     'ffn_norm_post': 2.83,
     'mix_norm_g_2': 3.315,
     'conv_b_pw1_2': 8.0,
     'conv_b_dw_2': 4.732,
     'conv_ln_g_2': 3.366,
     'conv_ln_b_2': 8.0,
     'conv_b_pw2_2': 5.994,
     'nsa_q_norm_2': 8.0,
     'nsa_kc_norm_2': 8.0,
     'nsa_ks_norm_2': 8.0,
     'nsa_kw_norm_2': 8.0,
     'nsa_pe_k_2': 8.0,
     'nsa_pe_v_2': 4.439,
     'ffn_b_dw_2': 7.938}
    for name, (base, spread) in spreads.items():
        noise = np.random.default_rng([zlib.crc32(name.encode()), seed]).standard_normal(out[name].shape)
        drawn = base * np.exp(spread * noise) if base else spread * noise
        out[name] = __import__('jax').numpy.asarray(drawn.astype(out[name].dtype))
    for name, factor in factors.items():
        out[name] = (out[name] * factor).astype(out[name].dtype)
    return out
```

```python
import math
from contextlib import ExitStack, contextmanager

import numpy as np

import concourse.bass as bass
from concourse import mybir

F32 = mybir.dt.float32
F32R = mybir.dt.float32r
ALU = mybir.AluOpType
ACT = mybir.ActivationFunctionType
AX_X = mybir.AxisListType.X

P = 128
T = 512
TB = T // P
D = 1024
DC = D // P
F = 2816
FC = F // P
EPS = 1e-6
BIG = -1e30
UC = 8

RH, RDK, RDV = 4, 256, 512
AH = 8
LAMBDA_INIT = 0.8 - 0.6 * math.exp(-0.3 * 1)
CW = 31
POOL_TAPS = 13
NH, NG, HD = 16, 4, 64
CL, CS = 32, 16
NCMP = (T - CL) // CS + 1
NP32 = 32
HID = 256

PHASES = ("retention", "ffn0", "diff", "ffn1", "conformer", "ffn2", "nsa", "ffn3")


class Turns:

    def __init__(self):
        self.n, self.base, self.was = 0, 0, None

    def take(self):
        n, self.n = self.n, self.n + 1
        return n % 2, self.base + n // 2

    def enter(self, i, per):
        assert per % 2 == 0
        self.was = (self.n, self.base)
        self.base = self.base + i * (per // 2)

    def leave(self, rounds, per):
        n, self.base = self.was
        assert self.n - n == per, (self.n - n, per)
        self.n = n + rounds * per


class Tally:

    def __init__(self, sem=None):
        self.sem, self.n, self.base, self.was = sem, 0, 0, None

    def next(self):
        self.n += 1
        return self.base + self.n

    def last(self):
        return self.base + self.n

    def enter(self, i, per):
        self.was = (self.n, self.base)
        self.base = self.base + i * per

    def leave(self, rounds, per):
        n, self.base = self.was
        assert self.n - n == per, (self.n - n, per)
        self.n = n + rounds * per


@contextmanager
def rounds(eng, count, *counted):
    with eng.Fori(0, count) as i:
        for counter, per in counted:
            counter.enter(i, per)
        yield i
    for counter, per in counted:
        counter.leave(count, per)


PARAM_ROWS = (
    ("a_norm_pre", D // P), ("a_norm_post", D // P), ("kv_norm", D // P), ("b_norm_pre", D // P),
    ("b_norm_post", D // P), ("ffn_norm_pre", 2 * DC), ("ffn_norm_post", 2 * DC),
    ("ffn_conv_w", 2 * 3 * 2 * FC), ("ffn_conv_b", 2 * 2 * FC), ("mix_norm_g_2", 2 * DC),
    ("ffn_norm_g_2", 2 * DC), ("conv_b_pw1_2", 2 * DC), ("conv_w_dw_2", CW * DC),
    ("conv_b_dw_2", DC), ("conv_ln_g_2", DC), ("conv_ln_b_2", DC), ("conv_b_pw2_2", DC),
    ("ffn_w_dw_2", 2 * 3 * FC), ("ffn_b_dw_2", 2 * FC), ("b_subln", 1),
    ("nsa_pe_k_2", CL * HD // P), ("nsa_pe_v_2", CL * HD // P),
    ("nsa_q_norm_2", 1), ("nsa_kc_norm_2", 1), ("nsa_ks_norm_2", 1), ("nsa_kw_norm_2", 1),
)
PARAM_AT = {}
_at = 0
for _name, _rows in PARAM_ROWS:
    PARAM_AT[_name] = _at
    _at += _rows
NPARAM = _at
PARAM_TILES = (NPARAM + P - 1) // P

CONST_AT = {}
_at = 0
for _name, _cols in (("ident", P), ("ones", P), ("halves", P), ("swap", P), ("causal", P)):
    CONST_AT[_name] = _at
    _at += _cols
NCONST = _at
RET_TABLE = 2 * T + RH * T
NSA_TABLE = 2 * T + 2 * TB * NP32


def tables():
    p, t = np.arange(P), np.arange(T)
    const = np.zeros((P, NCONST), np.float32)
    const[:, 0:P] = np.eye(P)
    const[:, P:2 * P] = 1.0
    const[:, 2 * P:3 * P] = (p[:, None] // HD == p[None, :] // HD)
    half = HD // 8
    for m in range(P):
        d = m % HD
        if d < 2 * half:
            const[m + half if d < half else m - half, 3 * P + m] = 1.0
    const[:, 4 * P:5 * P] = np.where(p[None, :] > p[:, None], BIG, 0.0)
    ret = np.zeros((P, RET_TABLE), np.float32)
    inv = (np.float32(1.0) / (np.float32(10000.0) ** np.linspace(0.0, 1.0, P, dtype=np.float32))).astype(np.float32)
    ang = (t.astype(np.float32)[None, :] * inv[:, None]).astype(np.float32)
    ret[:, 0:T], ret[:, T:2 * T] = np.cos(ang), np.sin(ang)
    for h in range(RH):
        lg = math.log1p(-2.0 ** (-5.0 - h))
        rel = t[None, :] - p[:, None]
        ret[:, (2 + h) * T:(3 + h) * T] = np.where(rel >= 0, np.exp(lg * np.maximum(rel, 0)), 0.0) * RDK ** -0.5
    nsa = np.zeros((P, NSA_TABLE), np.float32)
    inv = (np.float32(500000.0) ** (-np.arange(half, dtype=np.float32) * np.float32(2.0 / (2 * half)))).astype(np.float32)
    ang = (t.astype(np.float32)[None, :] * inv[:, None]).astype(np.float32)
    for m in range(P):
        d = m % HD
        nsa[m, 0:T] = np.cos(ang[d % half]) if d < 2 * half else 1.0
        if d < 2 * half:
            nsa[m, T:2 * T] = np.sin(ang[d % half]) * (-1.0 if d < half else 1.0)
    seen = np.zeros((P, TB, NP32), bool)
    for b in range(TB):
        seen[:, b, :NCMP] = (np.arange(NCMP)[None, :] * CS + CL - 1) <= (b * P + p[:, None])
    nsa[:, 2 * T:2 * T + TB * NP32] = seen.reshape(P, -1)
    nsa[:, 2 * T + TB * NP32:] = np.where(seen.reshape(P, -1), 0.0, BIG)
    return const, ret, nsa


def row_dmas(a, rows):
    found = []
    for name, n in PARAM_ROWS:
        at = PARAM_AT[name]
        v = a[name]
        if name in ("nsa_q_norm_2", "nsa_kc_norm_2", "nsa_ks_norm_2", "nsa_kw_norm_2"):
            for half in range(2):
                found.append((rows[at % P:at % P + 1, at // P, half * HD:(half + 1) * HD], v))
            continue
        letters = "abc"[:len(v.shape) - 1]
        flat = v.rearrange(f"{' '.join(letters)} n -> ({' '.join(letters)} n)") if letters else v
        flat = flat.rearrange("(r n) -> r n", n=P)
        done = 0
        while done < n:
            p, tile = (at + done) % P, (at + done) // P
            k = min(n - done, P - p)
            found.append((rows[p:p + k, tile, :], flat[done:done + k, :]))
            done += k
    return found


ROW_DMAS = 8 + sum((PARAM_AT[n] % P + r - 1) // P + 1 for n, r in PARAM_ROWS[:-4])


def program(nc, a, out, first=0, last=len(PHASES) - 1):
    run = [first <= n <= last for n in range(len(PHASES))]

    with ExitStack() as ctx:
        def sb(name, shape, dt=F32):
            return ctx.enter_context(nc.sbuf_tensor(name, shape, dt))

        def sem(name):
            return ctx.enter_context(nc.semaphore(name))

        x = sb("x", [P, DC, T])
        raw = [sb(f"raw{s}", [P, UC, P]) for s in range(2)]
        w_hi = [sb(f"w_hi{s}", [P, UC, P], F32R) for s in range(2)]
        w_lo = [sb(f"w_lo{s}", [P, UC, P], F32R) for s in range(2)]
        const = sb("const", [P, NCONST])
        params = sb("params", [P, PARAM_TILES * P])
        eps = sb("eps", [P, 1])
        sq = [sb(f"sq{s}", [P, T]) for s in range(2)]
        acc = sb("acc", [P, T])
        log_ms = sb("log_ms", [P, T])
        rs = sb("rs", [P, T])
        y = [sb(f"y{s}", [P, T]) for s in range(2)]
        xh = sb("xh", [P, DC, T], F32R)
        xl = sb("xl", [P, DC, T], F32R)

        def c_(name):
            return const[:, CONST_AT[name]:CONST_AT[name] + P]

        def col(name, k=0):
            at = PARAM_AT[name]
            return params[:, at + k:at + k + 1] if isinstance(k, int) else params[:, bass.ds(k + at, 1)]

        base = -(-nc.sbuf_base // 32) * 32
        room = nc.sbuf_usable_end - base
        nc_arena = ctx.enter_context(nc.sbuf_tensor("phase_memory", [P, room // 4 - 16], F32))
        del nc_arena

        class Map:

            def __init__(self, at=0):
                self.at = at

            def place(self, name, shape, dt=F32):
                t = nc.alloc_sbuf_tensor_at(name, shape, dt, offset=base + self.at)
                self.at += -(-4 * int(np.prod(shape[1:])) // 32) * 32
                assert self.at <= room - 64, (name, self.at, room)
                return t

        KB = 1024
        m = Map()
        x_in = m.place("x_in", [P, TB, D])
        rows = m.place("rows", [P, PARAM_TILES, P])
        x_out = m.place("x_out", [P, TB, D])

        m = Map()
        ffn_hi = m.place("ffn_hi", [P, FC, T], F32R)
        ffn_lo = m.place("ffn_lo", [P, FC, T], F32R)
        ffn_g = m.place("ffn_g", [P, T])
        ffn_u = m.place("ffn_u", [P, T])
        ffn_s = m.place("ffn_s", [P, T])
        ffn_p = m.place("ffn_p", [P, T])
        ffn_hT = m.place("ffn_hT", [P, DC, T])

        m = Map()
        ret_hi = m.place("ret_hi", [P, RH * RDV // P, T], F32R)
        ret_lo = m.place("ret_lo", [P, RH * RDV // P, T], F32R)
        ret_hT = Map(m.at).place("ret_hT", [P, DC, T])
        ret_tab = m.place("ret_tab", [P, RET_TABLE])
        ret_raw = m.place("ret_raw", [P, 2, T])
        ret_q = m.place("ret_q", [P, 2, T])
        ret_k = m.place("ret_k", [P, 2, T])
        ret_v = m.place("ret_v", [P, TB, RDV])
        ret_g = m.place("ret_g", [P, RDV // P, T])
        ret_o = m.place("ret_o", [P, RDV // P, T])
        ret_s23 = [m.place(f"ret_s{j}", [P, T - j * P]) for j in (2, 3)]
        ret_m = ret_o
        ret_s = [ret_raw[:, 0, :], ret_raw[:, 1, 0:T - P], ret_s23[0][:, :], ret_s23[1][:, :]]
        RC = RDV // P

        m = Map()
        att_hi = m.place("att_hi", [P, AH, T], F32R)
        att_lo = m.place("att_lo", [P, AH, T], F32R)
        dif_hT = Map(m.at).place("dif_hT", [P, DC, T])
        xqh = m.place("xqh", [P, DC, T], F32R)
        xql = m.place("xql", [P, DC, T], F32R)
        dif_k = m.place("dif_k", [P, 2, T])
        dif_q = m.place("dif_q", [P, 2, T])
        dif_v = m.place("dif_v", [P, 2, TB, P])
        dif_vt = m.place("dif_vt", [P, T])
        dif_e = m.place("dif_e", [P, 2, 2, T])
        dif_a = m.place("dif_a", [P, 2, T])
        dif_pt = m.place("dif_pt", [P, TB, T])
        dif_o = m.place("dif_o", [P, T])
        dif_lp = m.place("dif_lp", [P, 4 * 64])
        dif_lq = m.place("dif_lq", [P, 2, 64])
        dif_sm = m.place("dif_sm", [P, 32])
        lam_sum, lam_exp, neg_lam, sub_g = dif_sm[:, 0:2], dif_sm[:, 2:4], dif_sm[:, 4:5], dif_sm[:, 5:6]
        neg_max = dif_sm[:, 8:12].rearrange("p (s c) -> p s c", c=2)
        den = dif_sm[:, 12:16].rearrange("p (s c) -> p s c", c=2)
        inv_den = dif_sm[:, 16:20].rearrange("p (s c) -> p s c", c=2)

        m = Map()
        con_u = m.place("con_u", [P, CW - 1 + T])
        con_s = m.place("con_s", [P, T])
        con_a = m.place("con_a", [P, 3, T])
        con_t = m.place("con_t", [P, 2, T])
        con_y = m.place("con_y", [P, DC, T])
        con_mu = m.place("con_mu", [P, T])

        m = Map(2 * AH * T * 4)
        n_tabs = m.place("n_tabs", [P, NSA_TABLE])
        k_all = m.place("k_all", [P, 2, NG, T])
        v_all = m.place("v_all", [P, TB, 2, NG * HD])
        kc_all = m.place("kc_all", [P, NG * NCMP])
        vc_all = m.place("vc_all", [NP32, NG, HD])
        gates = m.place("gates", [P, TB, 3 * NH])
        n_raw = m.place("n_raw", [P, 2, T])
        n_t = m.place("n_t", [P, 2, T])
        q_gain = m.place("q_gain", [P, 8])
        m1 = Map(m.at)
        z = m1.place("z", [P, CL // 2, NG, NCMP])
        z_hi = [m1.place(f"z_hi{n}", [P, CL // 2, NG * NCMP], F32R) for n in "kv"]
        z_lo = [m1.place(f"z_lo{n}", [P, CL // 2, NG * NCMP], F32R) for n in "kv"]
        hid = m1.place("hid", [P, HID // P, NG * NCMP])
        hid_of = [[m1.place(f"hid_{n}{part}", [P, HID // P, NG * NCMP], F32R) for part in ("hi", "lo")] for n in "kv"]
        vc_t = n_raw[:, 1, 0:NG * NCMP]
        qn = m.place("qn", [P, 2, T])
        qr = m.place("qr", [P, 2, T])
        kst = m.place("kst", [P, 2, T])
        kcst = m.place("kcst", [P, NP32])
        vst = m.place("vst", [P, TB, 2, HD])
        vcst = m.place("vcst", [NP32, HD])
        n_e = m.place("n_e", [P, 2, 2, T])
        n_pt = m.place("n_pt", [P, 2, TB, T])
        ce = m.place("ce", [P, 8, NP32])
        pct = m.place("pct", [NP32, T])
        n_sm = m.place("n_sm", [P, 40])
        n_max, n_den, n_inv = (n_sm[:, k:k + 4].rearrange("p (s c) -> p s c", c=2) for k in (0, 4, 8))
        c_max, c_den = n_sm[:, 16:24], n_sm[:, 24:32]

        lin = [ctx.enter_context(nc.psum_tensor(f"lin{s}", [P, T], F32)) for s in range(2)]
        stat = ctx.enter_context(nc.psum_tensor("stat", [P, T], F32))
        trp = ctx.enter_context(nc.psum_tensor("trp", [P, TB, P], F32))
        att = ctx.enter_context(nc.psum_tensor("att", [P, 4, T], F32))

        raw_full = [sem(f"raw_full{s}") for s in range(2)]
        slot_taken = sem("slot_taken")
        hi_done = [sem(f"hi_done{s}") for s in range(2)]
        lo_done = [sem(f"lo_done{s}") for s in range(2)]
        unit_done = [sem(f"unit_done{s}") for s in range(2)]
        bank_free = [sem(f"bank_free{s}") for s in range(2)]
        x_ready = sem("x_ready")
        sq_ready = sem("sq_ready")
        sq_used = sem("sq_used")
        sum_done = sem("sum_done")
        acc_zero = sem("acc_zero")
        ln_done = sem("ln_done")
        rs_ready = sem("rs_ready")
        y_ready = sem("y_ready")
        xh_ready = sem("xh_ready")
        xl_ready = sem("xl_ready")
        t_ready = sem("t_ready")
        h_ready = sem("h_ready")
        const_in = sem("const_in")
        x_landed = sem("x_landed")
        rows_in = sem("rows_in")
        set_done = sem("set_done")
        tr_done = sem("tr_done")
        par_done = sem("par_done")
        xo_done = sem("xo_done")
        out_done = sem("out_done")
        eps_set = sem("eps_set")
        act_step = sem("act_step")
        dve_step = sem("dve_step")
        r_lo0 = sem("r_rot_half")
        f_tap = [sem(f"f_tap1_{n}") for n in "gu"]

        r_tab = sem("r_tab")
        r_raw = sem("r_raw")
        r_rot = sem("r_rot")
        r_vt = sem("r_vt")
        r_v = sem("r_v")
        r_g = sem("r_g")
        r_s = sem("r_s")
        r_sd = sem("r_sd")
        r_pv = sem("r_pv")
        r_o = sem("r_o")
        r_p = sem("r_p")
        r_hi = sem("r_hi")
        r_lo = sem("r_lo")
        d_lp = sem("d_lp")
        d_lam = sem("d_lam")
        d_k = sem("d_k")
        d_q = sem("d_q")
        d_vt = sem("d_vt")
        d_vr = sem("d_vr")
        d_v = sem("d_v")
        d_s = sem("d_s")
        d_mask = sem("d_mask")
        d_max = sem("d_max")
        d_e = sem("d_e")
        d_w = sem("d_w")
        d_a = sem("d_a")
        d_tr = sem("d_tr")
        d_pt = sem("d_pt")
        d_pv = sem("d_pv")
        d_o = sem("d_o")
        d_y = sem("d_y")
        d_hi = sem("d_hi")
        d_lo = sem("d_lo")
        c_sig = sem("c_sig")
        c_u = sem("c_u")
        c_tap = sem("c_tap")
        c_add = sem("c_add")
        c_own = sem("c_own")
        c_y = sem("c_y")
        c_sum = sem("c_sum")
        c_mu = sem("c_mu")
        c_ctr = sem("c_ctr")
        c_z = sem("c_z")
        c_pad = sem("c_pad")
        n_tab_in = sem("n_tab_in")
        n_z = sem("n_z")
        n_zh = sem("n_zh")
        n_zl = sem("n_zl")
        n_hid = sem("n_hid")
        n_hh = sem("n_hh")
        n_hl = sem("n_hl")
        n_rawd = sem("n_rawd")
        n_yn = sem("n_yn")
        n_sw = sem("n_sw")
        n_tt = sem("n_tt")
        n_kr = sem("n_kr")
        n_dup = sem("n_dup")
        n_qr = sem("n_qr")
        n_vt = sem("n_vt")
        n_vr = sem("n_vr")
        n_v = sem("n_v")
        n_gt = sem("n_gt")
        n_kc = sem("n_kc")
        n_vc = sem("n_vc")
        n_vcr = sem("n_vcr")
        n_vcd = sem("n_vcd")
        n_kst = sem("n_kst")
        n_vst = sem("n_vst")
        n_cs = sem("n_cs")
        n_c = sem("n_c")
        n_ce = sem("n_ce")
        n_tc = sem("n_tc")
        n_pc = sem("n_pc")
        n_s = sem("n_s")
        n_mask = sem("n_mask")
        n_mx = sem("n_mx")
        n_ex = sem("n_ex")
        n_w = sem("n_w")
        n_a = sem("n_a")
        n_tr = sem("n_tr")
        n_ptd = sem("n_ptd")
        n_pv = sem("n_pv")
        n_o = sem("n_o")
        n_lo = sem("n_lo")
        q_g = sem("q_g")
        f_cu = [sem(f"f_tap2_{n}") for n in "gu"]
        f_cv = [sem(f"f_conv_{n}") for n in "gu"]
        f_silu = sem("f_silu")
        f_prod = sem("f_prod")
        f_hi = sem("f_hi")
        f_lo = sem("f_lo")

        def w_cols(w, k0, kc, n):
            rows_ = w[k0 * P:(k0 + kc) * P, n:n + P] if isinstance(n, int) else w[k0 * P:(k0 + kc) * P, bass.ds(n, P)]
            return rows_.rearrange("(c p) n -> p c n", p=P)

        block = ctx.enter_context(nc.Block())

        @block.sync
        def _(sp):
            units = Turns()

            def load(src, kc=UC):
                s, t = units.take()
                sp.wait_ge(lo_done[s], t + 1)
                sp.sem_inc(slot_taken, 1)
                sp.dma_start(raw[s][:, 0:kc, :], src).then_inc(raw_full[s], 16)

            def project(w, kcs, outputs, column=0):
                with rounds(sp, outputs // 2, (units, 2 * len(kcs))) as i:
                    for o in range(2):
                        for n, kc in enumerate(kcs):
                            load(w_cols(w, UC * n, kc, i * (2 * P) + (o * P + column)), kc)

            def retention():
                w = a["a_w_in"][0]
                with rounds(sp, RH, (units, 12)) as h:
                    for base_, width in ((0, RDK), (RH * RDK, RDK), (2 * RH * RDK, RDV), (2 * RH * RDK + RH * RDV, RDV)):
                        for c in range(width // P):
                            load(w_cols(w, 0, UC, h * width + (base_ + c * P)))
                project(a["a_w_out"][0], (8, 8), DC)

            def ffn(w_up, w_down):
                with rounds(sp, FC, (units, 2)) as i:
                    load(w_cols(w_up, 0, UC, i * P))
                    load(w_cols(w_up, 0, UC, i * P + F))
                project(w_down, (8, 8, 6), DC)

            def nsa():
                w = a["nsa_w_in_2"][0]
                kv0 = NH * HD
                for c in range(4):
                    load(w_cols(w, 0, UC, kv0 + c * P))
                for first_ in (2 * NG * HD, 3 * NG * HD):
                    with rounds(sp, 2, (units, 2)) as i:
                        load(w_cols(w, 0, UC, i * (2 * NG * HD) + (kv0 + first_)))
                        load(w_cols(w, 0, UC, i * (2 * NG * HD) + (kv0 + first_ + P)))
                s, t = units.take()
                sp.wait_ge(lo_done[s], t + 1)
                sp.dma_start(raw[s][:, :, 0:3 * NH], w[:, kv0 + 6 * NG * HD:].rearrange("(c p) n -> p c n", p=P)).then_inc(raw_full[s], 16)
                for name in ("nsa_ck_w1_2", "nsa_cv_w1_2"):
                    for m_ in range(HID // P):
                        for k in range(2):
                            load(w_cols(a[name][0], UC * k, UC, m_ * P))
                for name in ("nsa_ck_w2_2", "nsa_cv_w2_2"):
                    s, t = units.take()
                    sp.wait_ge(lo_done[s], t + 1)
                    sp.dma_start(raw[s][:, 0:2, 0:HD], a[name][0].rearrange("(c p) n -> p c n", p=P)).then_inc(raw_full[s], 16)
                with rounds(sp, NH // 4, (units, 2)) as i:
                    load(w_cols(w, 0, UC, i * (2 * P)))
                    load(w_cols(w, 0, UC, i * (2 * P) + P))
                project(a["nsa_w_out_2"][0], (8,), DC)

            def conformer():
                with rounds(sp, DC, (units, 2)) as i:
                    load(w_cols(a["conv_w_pw1_2"][0], 0, UC, i * P + D))
                    load(w_cols(a["conv_w_pw1_2"][0], 0, UC, i * P))
                project(a["conv_w_pw2_2"][0], (8,), DC)

            def diff():
                def head(h):
                    load(w_cols(a["w_kv"], 0, UC, h * P))
                    load(w_cols(a["b_w_q"][0], 0, UC, h * P))
                    load(w_cols(a["w_kv"], 0, UC, h * P + D))
                head(0)
                with rounds(sp, AH // 2 - 1, (units, 6)) as i:
                    head(i * 2 + 1)
                    head(i * 2 + 2)
                head(AH - 1)
                project(a["b_w_out"][0], (8,), DC)

            if run[0]:
                retention()
            if run[1]:
                ffn(a["ffn_w_up"][0], a["ffn_w_down"][0])
            if run[2]:
                diff()
            if run[3]:
                ffn(a["ffn_w_up"][1], a["ffn_w_down"][1])
            if run[4]:
                conformer()
            if run[5]:
                ffn(a["ffn_w_up_2"][0], a["ffn_w_down_2"][0])
            if run[6]:
                nsa()
            if run[7]:
                ffn(a["ffn_w_up_2"][1], a["ffn_w_down_2"][1])
            o_v = out[0].rearrange("(b p) d -> p b d", p=P)
            for b in range(TB):
                sp.wait_ge(xo_done, 2 * (b + 1))
                sp.dma_start(o_v[:, b, :], x_out[:, b, :]).then_inc(out_done, 16)
            sp.wait_ge(out_done, 16 * TB)

        @block.gpsimd
        def _(pool):
            pre, upd = Tally(), Tally()

            pool.memset(eps[:, :], EPS).then_inc(eps_set, 1)

            def low_parts(hi=xh, lo=xl):
                for c in range(DC):
                    n = pre.next()
                    pool.wait_ge(xh_ready, n)
                    pool.tensor_tensor(lo[:, c, :], y[c % 2][:, :], hi[:, c, :].bitcast(F32), ALU.subtract).then_inc(xl_ready, 1)

            def add_update():
                for c in range(DC):
                    pool.wait_ge(t_ready, upd.next())
                    pool.tensor_tensor(x[:, c, :], x[:, c, :], y[c % 2][:, :], ALU.add).then_inc(x_ready, 1)

            for n in (0, 1):
                if run[n]:
                    low_parts()
                    add_update()
            if run[2]:
                low_parts()
                low_parts(xqh, xql)
                add_update()
            if run[3]:
                low_parts()
                add_update()
            if run[4]:
                low_parts()
                cn, cp = Tally(), Tally()
                with rounds(pool, DC, (cn, 1)):
                    n = cn.next()
                    for k in range(1, POOL_TAPS):
                        pool.wait_ge(c_tap, (n - 1) * POOL_TAPS + k + 1)
                        if k > 1:
                            pool.wait_ge(c_add, (n - 1) * (POOL_TAPS - 1) + k - 1)
                        pool.tensor_tensor(con_a[:, 2, :], con_a[:, 2, :], con_t[:, k % 2, :], ALU.add).then_inc(c_add, 1)
                for c in range(DC):
                    n = pre.next()
                    pool.wait_ge(xh_ready, n)
                    pool.tensor_tensor(xl[:, c, :], con_t[:, c % 2, :], xh[:, c, :].bitcast(F32), ALU.subtract).then_inc(xl_ready, 1)
            if run[5]:
                low_parts()
            if run[6]:
                low_parts()
            if run[7]:
                low_parts()

        @block.tensor
        def _(pe):
            units, banks, squares, sums, pre = Turns(), Turns(), Tally(), Tally(), Tally()
            heads, r_scores, r_outs = Tally(), Tally(), Tally()

            def parts(hi, lo, k):
                return hi[:, k, :], lo[:, k, :]

            def unit(bank, hi, lo, k0, kc, start, stop, fresh=None):
                s, t = units.take()
                pe.wait_ge(lo_done[s], t + 2)
                for k in range(kc):
                    if fresh is not None:
                        pe.wait_ge(*fresh(k))
                    h, l = parts(hi, lo, k0 + k)
                    pe.matmul(bank, w_hi[s][:, k, :], h, start=start and k == 0, stop=False)
                    pe.matmul(bank, w_hi[s][:, k, :], l, start=False, stop=False)
                    done = pe.matmul(bank, w_lo[s][:, k, :], h, start=False, stop=stop and k == kc - 1)
                done.then_inc(unit_done[s], 1)

            def output(hi, lo, kcs, fresh=None, cols=T):
                b, t = banks.take()
                pe.wait_ge(bank_free[b], t + 1)
                for n, kc in enumerate(kcs):
                    unit(lin[b][:, 0:cols], hi, lo, UC * n, kc, n == 0, n == len(kcs) - 1,
                         None if fresh is None else lambda k, n=n: fresh(UC * n + k))
                return b

            def sum_square(start, stop):
                v = squares.next()
                pe.wait_ge(sq_ready, v)
                pe.matmul(stat[:, :], c_("ones"), sq[(squares.n - 1) % 2][:, :], start=start, stop=stop).then_inc(sq_used, 1)

            def norm_x(copies=1):
                for c in range(DC):
                    sum_square(c == 0, c == DC - 1)
                first_ = pre.n
                for c in range(DC * copies):
                    pre.next()
                return lambda k: (xl_ready, first_ + k + 1)

            def project(hi, lo, kcs, outputs, fresh=None):
                with rounds(pe, outputs // 2, (units, 2 * len(kcs)), (banks, 2)):
                    for o in range(2):
                        output(hi, lo, kcs, fresh if o == 0 else None)

            def sum_acc():
                for c in range(DC):
                    squares.next()
                pe.wait_ge(sq_used, squares.last())
                pe.matmul(stat[:, :], c_("ones"), acc[:, :], start=True, stop=True).then_inc(sum_done, 1)

            def retention():
                xs = norm_x()
                vt, vd, gs = Tally(), Tally(), Tally()
                with rounds(pe, RH, (units, 12), (banks, 12), (squares, RC), (heads, 1), (vt, RC), (vd, RC),
                            (r_scores, TB), (r_outs, RC)):
                    h = heads.next()
                    for n in range(4):
                        output(xh, xl, (UC,), xs if n == 0 else None)

                    def turn_v(c):
                        pe.wait_ge(r_raw, h * 8 - 8 + 4 + c + 1)
                        v = vt.next()
                        pe.wait_ge(r_v, v)
                        for b in range(TB):
                            done = pe.transpose(trp[:, b, :], ret_raw[:, c % 2, b * P:(b + 1) * P], c_("ident"))
                        done.then_inc(r_vt, 1)

                    for c in range(RC):
                        output(xh, xl, (UC,))
                        if c:
                            turn_v(c - 1)
                    output(xh, xl, (UC,))
                    turn_v(RC - 1)
                    output(xh, xl, (UC,))
                    pe.wait_ge(r_rot, h * 2)
                    for j in range(TB):
                        for d in range(2):
                            done = pe.matmul(att[:, j, 0:T - j * P], ret_k[:, d, j * P:(j + 1) * P], ret_q[:, d, j * P:],
                                             start=d == 0, stop=d == 1)
                        done.then_inc(r_s, 1)
                    output(xh, xl, (UC,))
                    for c in range(RC):
                        pe.wait_ge(r_v, h * RC + 1)
                        for j in range(TB):
                            pe.wait_ge(r_sd, h * TB) if c == 0 and j == 0 else None
                            done = pe.matmul(att[:, c, j * P:], ret_v[:, j, c * P:(c + 1) * P], ret_s[j],
                                             start=j == 0, stop=j == TB - 1)
                        done.then_inc(r_pv, 1)
                    output(xh, xl, (UC,))
                    for c in range(RC):
                        sum_square(c == 0, c == RC - 1)
                    for c in range(RC):
                        vd.next(), r_scores.next(), r_outs.next()
                project(ret_hi, ret_lo, (8, 8), DC, lambda k: (r_lo, (RH * RC)))
                sum_acc()

            def head_sums(b, cols=T):
                v = squares.next()
                pe.wait_ge(sq_ready, v)
                pe.matmul(lin[b][:, 0:cols], c_("halves"), sq[(squares.n - 1) % 2][:, 0:cols], start=True, stop=True).then_inc(sq_used, 1)

            ropes, steps = Tally(), Tally()

            def partners(b, src):
                v = ropes.next()
                pe.wait_ge(n_yn, v)
                pe.matmul(lin[b][:, :], c_("swap"), src, start=True, stop=True).then_inc(n_sw, 1)

            def nsa():
                xs = norm_x()
                for c in range(4):
                    output(xh, xl, (UC,), xs)
                with rounds(pe, 2, (units, 2), (banks, 2), (squares, 2), (ropes, 2)):
                    bs = [output(xh, xl, (UC,)) for _ in range(2)]
                    for b in bs:
                        head_sums(b)
                        partners(b, y[0][:, :])
                vt = Tally()
                with rounds(pe, 2, (units, 2), (banks, 2), (vt, 2)):
                    for _ in range(2):
                        output(xh, xl, (UC,))
                    for c in range(2):
                        n = vt.next()
                        pe.wait_ge(n_vt, n)
                        if c:
                            pe.wait_ge(n_v, n - 1)
                        for k in range(TB):
                            done = pe.transpose(trp[:, k, :], n_raw[:, c, k * P:(k + 1) * P], c_("ident"))
                        done.then_inc(n_vr, 1)
                s, t = units.take()
                b, bt = banks.take()
                pe.wait_ge(lo_done[s], t + 2)
                pe.wait_ge(bank_free[b], bt + 1)
                for k in range(TB):
                    dst, r = lin[b][:, k * 3 * NH:(k + 1) * 3 * NH], slice(k * P, (k + 1) * P)
                    for c in range(UC):
                        pe.matmul(dst, xh[:, c, r], w_hi[s][:, c, 0:3 * NH], start=c == 0, stop=False)
                        pe.matmul(dst, xl[:, c, r], w_hi[s][:, c, 0:3 * NH], start=False, stop=False)
                        done = pe.matmul(dst, xh[:, c, r], w_lo[s][:, c, 0:3 * NH], start=False, stop=c == UC - 1)
                done.then_inc(unit_done[s], 1)
                for n in range(2):
                    for m_ in range(HID // P):
                        output(z_hi[n], z_lo[n], (UC, UC), lambda k, n=n: (n_zl, n + 1), NG * NCMP)
                    if n == 0:
                        continue
                for n in range(2):
                    b = output(hid_of[n][0], hid_of[n][1], (HID // P,), lambda k, n=n: (n_hl, 2 * n + 2), NG * NCMP)
                    if n == 0:
                        head_sums(b, NG * NCMP)
                pe.wait_ge(n_vc, 1)
                for g in range(NG):
                    done = pe.transpose(trp[0:NCMP, g, 0:HD], vc_t[0:HD, g * NCMP:(g + 1) * NCMP], c_("ident")[0:HD, 0:HD])
                done.then_inc(n_vcr, 1)

                def block_scores(p, n, it):
                    hh, blk, sl = it // TB, it % TB, it % 2
                    r, w = slice(hh * HD, (hh + 1) * HD), (blk + 1) * P
                    for br in range(2):
                        done = pe.matmul(att[:, 2 * sl + br, 0:w], qr[r, p, blk * P:w], kst[r, br, 0:w], start=True, stop=True)
                    done.then_inc(n_s, 1)

                def turn(n, it):
                    pe.wait_ge(n_a, (n - 1) * 8 + it + 1)
                    if it:
                        pe.wait_ge(n_ptd, (n - 1) * 16 + 2 * it)
                    for br in range(2):
                        for k in range(it % TB + 1):
                            dst = trp[:, k, :] if br == 0 else stat[:, k * P:(k + 1) * P]
                            done = pe.transpose(dst, n_e[:, it % 2, br, k * P:(k + 1) * P], c_("ident"))
                        done.then_inc(n_tr, 1)

                def turn_compressed(n, hh):
                    for k in range(TB):
                        done = pe.transpose(trp[0:NCMP, k, :], ce[:, hh * TB + k, 0:NCMP], c_("ident"))
                    done.then_inc(n_tc, 1)

                def weigh(n, hh, bo):
                    r = slice(hh * HD, (hh + 1) * HD)
                    pe.wait_ge(n_ptd, (n - 1) * 16 + 8 * (hh + 1))
                    for br in range(2):
                        for k in range(TB):
                            pe.matmul(lin[bo][r, k * P:], vst[:, k, br, :], n_pt[:, br, k, k * P:], start=br == 0 and k == 0, stop=False)
                    pe.wait_ge(n_pc, (n - 1) * 2 + hh + 1)
                    pe.matmul(lin[bo][r, :], vcst[0:NCMP, :], pct[0:NCMP, :], start=False, stop=True).then_inc(n_pv, 1)

                def step(p, more):
                    n = steps.next()
                    bo, bt = banks.take()
                    pe.wait_ge(bank_free[bo], bt + 1)
                    pe.wait_ge(n_kst, 2 * ((n + 1) // 2) if isinstance(n, int) else group_of(n, p))
                    pe.wait_ge(n_qr, n)
                    for hh in range(2):
                        r = slice(hh * HD, (hh + 1) * HD)
                        for k in range(TB):
                            dst = (lin[bo], stat)[hh][:, k * NP32:k * NP32 + NCMP]
                            done = pe.matmul(dst, qn[r, p, k * P:(k + 1) * P], kcst[r, 0:NCMP], start=True, stop=True)
                    done.then_inc(n_cs, 1)
                    block_scores(p, n, 0)
                    block_scores(p, n, 1)
                    if more:
                        b = output(xh, xl, (UC,))
                        head_sums(b)
                    pe.wait_ge(n_c, (n - 1) * 10 + 10)
                    for it in (0, 1):
                        turn(n, it)
                        pe.wait_ge(n_ex, (n - 1) * 16 + 2 * (it + 1))
                        block_scores(p, n, it + 2)
                    pe.wait_ge(n_ptd, (n - 1) * 16 + 4)
                    turn_compressed(n, 0)
                    if more:
                        partners(b, qn[:, 1 - p, :])
                    pe.wait_ge(n_pc, (n - 1) * 2 + 1)
                    for it in (2, 3):
                        turn(n, it)
                        pe.wait_ge(n_ex, (n - 1) * 16 + 2 * (it + 1))
                        block_scores(p, n, it + 2)
                    pe.wait_ge(n_vst, 2 * ((n + 1) // 2) if isinstance(n, int) else group_of(n, p))
                    weigh(n, 0, bo)
                    turn_compressed(n, 1)
                    pe.wait_ge(n_pc, (n - 1) * 2 + 2)
                    for it in (4, 5):
                        turn(n, it)
                        pe.wait_ge(n_ex, (n - 1) * 16 + 2 * (it + 1))
                        block_scores(p, n, it + 2)
                    turn(n, 6)
                    turn(n, 7)
                    weigh(n, 1, bo)

                def group_of(n, p):
                    return n + (1 - p)

                b = output(xh, xl, (UC,))
                head_sums(b)
                partners(b, qn[:, 0, :])
                with rounds(pe, NG - 1, (units, 2), (banks, 4), (squares, 2), (ropes, 2), (steps, 2)):
                    step(0, True)
                    step(1, True)
                step(0, True)
                step(1, False)
                project(att_hi, att_lo, (8,), DC, lambda k: (n_lo, k + 1))

            def conformer():
                xs = norm_x()
                with rounds(pe, DC, (units, 2), (banks, 2)):
                    output(xh, xl, (UC,), xs)
                    output(xh, xl, (UC,))
                for c in range(DC):
                    pe.wait_ge(c_y, c + 1)
                    pe.matmul(stat[:, :], c_("ones"), con_y[:, c, :], start=c == 0, stop=c == DC - 1).then_inc(c_sum, 1)
                pe.wait_ge(c_mu, 1)
                project(xh, xl, (UC,), DC, norm_x())

            hd = Tally()

            def diff():
                xs = norm_x(2)

                def turn_v(n):
                    pe.wait_ge(d_vt, n)
                    for b in range(TB):
                        done = pe.transpose(trp[:, b, :], dif_vt[:, b * P:(b + 1) * P], c_("ident"))
                    done.then_inc(d_vr, 1)

                def score(p, n, b):
                    s, w = b % 2, (b + 1) * P
                    for c in range(2):
                        r = slice(c * 64, c * 64 + 64)
                        done = pe.matmul(att[:, 2 * s + c, 0:w], dif_q[r, p, b * P:(b + 1) * P], dif_k[r, p, 0:w],
                                         start=True, stop=True)
                    done.then_inc(d_s, 1)

                def turn(n, b):
                    pe.wait_ge(d_a, (n - 1) * TB + b + 3)
                    for k in range(b + 1):
                        done = pe.transpose(trp[:, k, :], dif_a[:, b % 2, k * P:(k + 1) * P], c_("ident"))
                    done.then_inc(d_tr, 1)

                def step(p, more):
                    n = hd.next()
                    pe.wait_ge(d_k, n)
                    pe.wait_ge(d_q, n)
                    score(p, n, 0)
                    pe.wait_ge(d_o, n)
                    score(p, n, 1)
                    if more:
                        output(xh, xl, (UC,))
                    turn(n, 0)
                    pe.wait_ge(d_pt, (n - 1) * TB + 1)
                    turn(n, 1)
                    for b in (2, 3):
                        pe.wait_ge(d_e, (n - 1) * 2 * TB + 2 * (b - 1))
                        score(p, n, b)
                    if more:
                        output(xqh, xql, (UC,))
                    pe.wait_ge(d_pt, (n - 1) * TB + 2)
                    turn(n, 2)
                    pe.wait_ge(d_pt, (n - 1) * TB + 3)
                    turn(n, 3)
                    pe.wait_ge(d_v, n)
                    pe.wait_ge(d_pt, n * TB)
                    for k in range(TB):
                        done = pe.matmul(att[:, 3, k * P:], dif_v[:, p, k, :], dif_pt[:, k, k * P:], start=k == 0, stop=k == TB - 1)
                    done.then_inc(d_pv, 1)
                    if more:
                        output(xh, xl, (UC,))
                        turn_v(n + 1)
                    sum_square(True, True)

                output(xh, xl, (UC,), xs)
                output(xqh, xql, (UC,), lambda k: (xs(k)[0], xs(k)[1] + DC))
                output(xh, xl, (UC,))
                turn_v(1)
                with rounds(pe, AH // 2 - 1, (units, 6), (banks, 6), (squares, 2), (hd, 2)):
                    step(0, True)
                    step(1, True)
                step(0, True)
                step(1, False)
                project(att_hi, att_lo, (8,), DC, lambda k: (d_lo, k + 1))
                sum_acc()

            n_ffn = [0]

            def ffn(post):
                xs = norm_x()
                with rounds(pe, FC, (units, 2), (banks, 2)):
                    output(xh, xl, (UC,), xs)
                    output(xh, xl, (UC,))
                n_ffn[0] += 1
                done_ = n_ffn[0] * FC
                project(ffn_hi, ffn_lo, (8, 8, 6), DC, lambda k: (f_lo, done_ - FC + k + 1))
                if post:
                    sum_acc()

            pe.wait_ge(const_in, 16)
            for c in range(DC):
                if c == 0:
                    pe.wait_ge(x_landed, 16)
                if c >= 4:
                    pe.wait_ge(x_ready, c - 3)
                for b in range(TB):
                    done = pe.transpose(att[:, c % 4, b * P:(b + 1) * P], x_in[:, b, c * P:(c + 1) * P], c_("ident"))
                done.then_inc(tr_done, 1)
            pe.wait_ge(rows_in, ROW_DMAS * 16)
            for r in range(PARAM_TILES):
                n = min(P, NPARAM - r * P)
                if r % 4 == 0 and r:
                    pe.wait_ge(par_done, 1)
                done = pe.transpose(trp[:, r % 4, 0:n], rows[0:n, r, :], c_("ident")[0:n, 0:n])
                if r % 4 == 3 or r == PARAM_TILES - 1:
                    done.then_inc(tr_done, 1)
            if run[0]:
                retention()
            if run[1]:
                ffn(True)
            if run[2]:
                diff()
            if run[3]:
                ffn(True)
            if run[4]:
                conformer()
            if run[5]:
                ffn(False)
            if run[6]:
                nsa()
            if run[7]:
                ffn(False)
            pe.wait_ge(x_ready, (1 + sum(run)) * DC)
            for b in range(TB):
                for half in range(2):
                    n = 2 * b + half
                    if n >= 4:
                        pe.wait_ge(xo_done, n - 3)
                    for k in range(4):
                        done = pe.transpose(att[:, n % 4, k * P:(k + 1) * P], x[:, 4 * half + k, b * P:(b + 1) * P], c_("ident"))
                    done.then_inc(tr_done, 1)

        @block.scalar
        def _(act):
            units, banks, squares, sums, rss, accs = Turns(), Turns(), Tally(), Tally(), Tally(), Tally()
            pre, upd, own, hs = Tally(), Tally(), Tally(), Tally()

            def split_next(last_ones=False, twice=False):
                s, t = units.take()
                act.wait_ge(unit_done[s], t + 1)
                if twice:
                    act.wait_ge(raw_full[s], (t + 2) * 16)
                    act.activation(w_hi[s][:, 0:2, :].rearrange("p c (r n) -> p c r n", r=2),
                                   raw[s][:, 0:2, 0:HD].unsqueeze(2).broadcast_to([P, 2, 2, HD]), ACT.Copy).then_inc(hi_done[s], 1)
                elif not last_ones:
                    act.wait_ge(raw_full[s], (t + 2) * 16)
                    act.activation(w_hi[s][:, :, :], raw[s][:, :, :], ACT.Copy).then_inc(hi_done[s], 1)

            def square(src, scale=1.0, cols=T):
                v = squares.next()
                if squares.n > 2 or not isinstance(v, int):
                    act.wait_ge(sq_used, v - 2)
                act.activation(sq[(squares.n - 1) % 2][:, 0:cols], src, ACT.Square, scale=scale).then_inc(sq_ready, 1)

            def inverse_rms(n, src=None, cols=T):
                v = rss.next()
                src = stat if src is None else src
                act.activation(log_ms[:, 0:cols], src[:, 0:cols], ACT.Ln, scale=1.0 / n, bias=eps[:, :]).then_inc(ln_done, 1)
                act.wait_ge(ln_done, v)
                act.activation(rs[:, 0:cols], log_ms[:, 0:cols], ACT.Exp, scale=-0.5).then_inc(rs_ready, 1)

            def norm_x(his=(xh,)):
                for c in range(DC):
                    act.wait_ge(x_ready, upd.n * DC + c + 1)
                    square(x[:, c, :])
                act.wait_ge(sq_used, squares.last())
                inverse_rms(D)
                for hi in his:
                    for c in range(DC):
                        act.wait_ge(y_ready, pre.next())
                        act.activation(hi[:, c, :], y[c % 2][:, :], ACT.Copy).then_inc(xh_ready, 1)

            def project_out(hT, nu, final=False):
                def one(o, k, no_more):
                    for n in range(nu):
                        split_next(no_more and o * nu + n >= 2 * nu - 2)
                    b, t = banks.take()
                    square(lin[b][:, :])
                    act.activation(hT[:, k, :] if isinstance(k, int) else hT[:, bass.ds(k, 1), :], lin[b][:, :], ACT.Copy).then_inc(bank_free[b], 1)

                n_loop = DC // 2 - (1 if final else 0)
                with rounds(act, n_loop, (units, 2 * nu), (banks, 2), (squares, 2)) as i:
                    for o in range(2):
                        one(o, i * 2 + o, False)
                if final:
                    for o in range(2):
                        one(o, DC - 2 + o, True)
                act.wait_ge(sum_done, accs.next())
                inverse_rms(D)

            def residual_out(nu, final=False):
                n_loop = DC // 2 - (1 if final else 0)
                with rounds(act, n_loop, (units, 2 * nu)):
                    for o in range(2 * nu):
                        split_next()
                if final:
                    for o in range(2 * nu):
                        split_next(o >= 2 * nu - 2)
                for o in range(DC):
                    banks.take()

            r_raws, r_gs, r_oo, heads = Tally(), Tally(), Tally(), Tally()

            def retention(final):
                norm_x()
                with rounds(act, RH, (units, 12), (banks, 12), (squares, RC), (rss, 1), (r_raws, 8), (r_gs, RC), (heads, 1)) as i:
                    h = heads.next()

                    def bank_out(dst, func, ready, value):
                        split_next()
                        b, t = banks.take()
                        act.activation(dst, lin[b][:, :], func).then_inc(ready, 1)
                        act.wait_ge(ready, value)
                        act.sem_inc(bank_free[b], 1)

                    for n in range(4):
                        if n == 2:
                            act.wait_ge(r_rot, h * 2 - 1)
                        bank_out(ret_raw[:, n % 2, :], ACT.Copy, r_raw, (h - 1) * 8 + n + 1)

                    def place_v(c):
                        act.wait_ge(r_vt, (h - 1) * RC + c + 1)
                        act.activation(ret_v[:, :, c * P:(c + 1) * P], trp[:, :, :], ACT.Copy).then_inc(r_v, 1)

                    for c in range(RC):
                        if c == 0:
                            act.wait_ge(r_rot, h * 2)
                        bank_out(ret_raw[:, c % 2, :], ACT.Copy, r_raw, (h - 1) * 8 + 5 + c)
                        if c:
                            place_v(c - 1)
                    bank_out(ret_g[:, 0, :], ACT.Silu, r_g, (h - 1) * RC + 1)
                    place_v(RC - 1)
                    bank_out(ret_g[:, 1, :], ACT.Silu, r_g, (h - 1) * RC + 2)
                    bank_out(ret_g[:, 2, :], ACT.Silu, r_g, (h - 1) * RC + 3)
                    for c in range(RC):
                        act.wait_ge(r_pv, (h - 1) * RC + c + 1)
                        act.activation(ret_o[:, c, :], att[:, c, :], ACT.Copy).then_inc(r_o, 1)
                    bank_out(ret_g[:, 3, :], ACT.Silu, r_g, (h - 1) * RC + 4)
                    for c in range(RC):
                        act.wait_ge(r_o, (h - 1) * RC + c + 1)
                        square(ret_o[:, c, :])
                    act.wait_ge(sq_used, squares.last())
                    inverse_rms(RDV)
                    for c in range(RC):
                        act.wait_ge(r_p, (h - 1) * 2 * RC + 2 * c + 2)
                        act.activation(ret_hi[:, bass.ds(i * RC + c, 1), :], y[c % 2][:, :], ACT.Copy).then_inc(r_hi, 1)
                    for _ in range(8):
                        r_raws.next()
                    for _ in range(RC):
                        r_gs.next()
                project_out(ret_hT, 2, final)
                upd.next()

            steps, ropes = Tally(), Tally()

            def nsa(final):
                norm_x()
                NC = NG * NCMP
                for n in range(2):
                    for _ in range(2):
                        split_next()
                        banks.take()
                    act.wait_ge(n_z, 16 * (n + 1))
                    act.activation(z_hi[n][:, :, :], z[:, :, :, :].rearrange("p l g n -> p l (g n)"), ACT.Copy).then_inc(n_zh, 1)

                def copy_norm(k):
                    split_next()
                    b, t = banks.take()
                    act.activation(n_raw[:, k, :], lin[b][:, :], ACT.Copy).then_inc(n_rawd, 1)
                    square(lin[b][:, :])
                    return b

                def head_rms(b, last_sq):
                    act.wait_ge(sq_used, last_sq)
                    inverse_rms(HD, lin[b])

                with rounds(act, 2, (units, 2), (banks, 2), (squares, 2), (rss, 2), (ropes, 2)) as i:
                    bs = [copy_norm(0), copy_norm(1)]
                    for c in range(2):
                        n = ropes.next()
                        if c:
                            act.wait_ge(n_yn, n - 1)
                        head_rms(bs[c], squares.last() - 1 + c)
                    for c in range(2):
                        n = ropes.last() - 1 + c
                        act.wait_ge(n_kr, 2 * n)
                        for half in range(2):
                            here, there = slice(half * HD, half * HD + HD), slice(HD - half * HD, 2 * HD - half * HD)
                            act.activation(k_all[there, bass.ds(i, 1), 2 * c + half, :], k_all[here, bass.ds(i, 1), 2 * c + half, :],
                                           ACT.Copy).then_inc(n_dup, 1)
                vt = Tally()
                with rounds(act, 2, (units, 2), (banks, 2), (vt, 2)) as i:
                    for c in range(2):
                        split_next()
                        b, t = banks.take()
                        v = vt.next()
                        act.activation(n_raw[:, c, :], lin[b][:, :], ACT.Copy).then_inc(n_vt, 1)
                        act.wait_ge(n_vt, v)
                        act.sem_inc(bank_free[b], 1)
                    for c in range(2):
                        act.wait_ge(n_vr, vt.last() - 1 + c)
                        act.activation(v_all[:, :, bass.ds(i, 1), c * P:(c + 1) * P], trp[:, :, :].unsqueeze(2), ACT.Copy).then_inc(n_v, 1)
                split_next()
                b, t = banks.take()
                act.activation(gates[:, :, :], lin[b][:, 0:TB * 3 * NH].rearrange("p (b n) -> p b n", b=TB), ACT.Sigmoid).then_inc(n_gt, 1)
                act.wait_ge(n_gt, 1)
                act.sem_inc(bank_free[b], 1)
                for n in range(2):
                    for m_ in range(HID // P):
                        w2_next = n == 1 and m_ == 1
                        split_next(twice=w2_next)
                        split_next(twice=w2_next)
                        b, t = banks.take()
                        v = 2 * n + m_ + 1
                        act.activation(hid[:, m_, :], lin[b][:, 0:NC], ACT.Silu).then_inc(n_hid, 1)
                        act.wait_ge(n_hid, v)
                        act.sem_inc(bank_free[b], 1)
                        act.activation(hid_of[n][0][:, m_, :], hid[:, m_, :], ACT.Copy).then_inc(n_hh, 1)
                        act.wait_ge(n_hl, v)
                split_next()
                b, t = banks.take()
                act.activation(n_raw[:, 0, 0:NC], lin[b][:, 0:NC], ACT.Copy).then_inc(n_kc, 1)
                square(lin[b][:, 0:NC], cols=NC)
                act.wait_ge(sq_used, squares.last())
                inverse_rms(HD, lin[b], NC)
                act.wait_ge(rs_ready, rss.last())
                act.sem_inc(bank_free[b], 1)
                split_next()
                b, t = banks.take()
                act.activation(vc_t, lin[b][:, 0:NC], ACT.Copy).then_inc(n_vc, 1)
                act.wait_ge(n_vc, 1)
                act.sem_inc(bank_free[b], 1)
                act.wait_ge(n_vcr, 1)
                act.activation(vc_all[0:NCMP, :, :], trp[0:NCMP, :, 0:HD], ACT.Copy).then_inc(n_vcd, 1)

                def stage(g):
                    act.activation(kst[:, :, :].unsqueeze(2), k_all[:, :, bass.ds(g, 1), :] if not isinstance(g, int) else k_all[:, :, g:g + 1, :],
                                   ACT.Copy).then_inc(n_kst, 1)
                    act.activation(kcst[:, 0:NCMP], kc_all[:, bass.ds(g * NCMP, NCMP)] if not isinstance(g, int) else kc_all[:, g * NCMP:(g + 1) * NCMP],
                                   ACT.Copy).then_inc(n_kst, 1)

                def exps(n, it):
                    sl, w = it % 2, (it % TB + 1) * P
                    act.wait_ge(n_mx, (n - 1) * 8 + it + 1)
                    act.wait_ge(n_tr, (n - 1) * 16 + 2 * it + 2)
                    for br in range(2):
                        act.activation(n_e[:, sl, br, 0:w], att[:, 2 * sl + br, 0:w], ACT.Exp, bias=n_max[:, sl, br:br + 1],
                                       accum_out=n_den[:, sl, br:br + 1]).then_inc(n_ex, 1)

                def place(n, it):
                    blk = it % TB
                    for br in range(2):
                        act.wait_ge(n_tr, (n - 1) * 16 + 2 * it + br + 5)
                        src = trp[:, 0:blk + 1, :] if br == 0 else stat[:, 0:(blk + 1) * P].rearrange("p (k q) -> p k q", q=P)
                        act.activation(n_pt[:, br, 0:blk + 1, blk * P:(blk + 1) * P], src, ACT.Copy).then_inc(n_ptd, 1)

                def place_compressed(n, hh):
                    act.wait_ge(n_tc, (n - 1) * 2 + hh + 1)
                    act.activation(pct[0:NCMP, :], trp[0:NCMP, :, :].rearrange("p k q -> p (k q)"), ACT.Copy).then_inc(n_pc, 1)

                def step(p, more):
                    n = steps.next()
                    bo, bt = banks.take()
                    act.wait_ge(n_c, (n - 1) * 10 + 4)
                    act.activation(ce[:, :, 0:NCMP], ce[:, :, 0:NCMP], ACT.Exp).then_inc(n_ce, 1)
                    exps(n, 0)
                    exps(n, 1)
                    if more:
                        b = copy_norm(1 - p)
                        head_rms(b, squares.last())
                    for it in (0, 1):
                        place(n, it)
                        exps(n, it + 2)
                    place_compressed(n, 0)
                    for it in (2, 3):
                        place(n, it)
                        exps(n, it + 2)
                    place_compressed(n, 1)
                    for it in (4, 5):
                        place(n, it)
                        exps(n, it + 2)
                    place(n, 6)
                    place(n, 7)
                    act.wait_ge(n_pv, 2 * n)
                    k = slice(n - 1, n) if isinstance(n, int) else bass.ds(n - 1, 1)
                    act.activation(att_hi[:, k, :], lin[bo][:, :].unsqueeze(1), ACT.Copy).then_inc(n_o, 1)

                act.wait_ge(n_kc, 2)
                b = copy_norm(0)
                head_rms(b, squares.last())
                with rounds(act, NG - 1, (units, 2), (banks, 4), (squares, 2), (rss, 2), (steps, 2)) as g:
                    stage(g)
                    step(0, True)
                    step(1, True)
                stage(NG - 1)
                step(0, True)
                step(1, False)
                residual_out(1, final)
                upd.next()

            def conformer(final):
                norm_x()
                cn = Tally()
                with rounds(act, DC, (units, 2), (banks, 2), (cn, 1)) as i:
                    n = cn.next()
                    split_next()
                    b, t = banks.take()
                    act.activation(con_s[:, :], lin[b][:, :], ACT.Sigmoid, bias=col("conv_b_pw1_2", i + DC)).then_inc(c_sig, 1)
                    act.wait_ge(c_sig, n)
                    act.sem_inc(bank_free[b], 1)
                    split_next()
                    banks.take()
                    act.wait_ge(c_u, n)
                    for k in range(POOL_TAPS):
                        j = CW - 1 - k
                        if k > 2:
                            act.wait_ge(c_add, (n - 1) * (POOL_TAPS - 1) + k - 2)
                        act.activation(con_t[:, k % 2, :] if k else con_a[:, 2, :], con_u[:, j:j + T], ACT.Copy,
                                       scale=col("conv_w_dw_2", i + j * DC)).then_inc(c_tap, 1)
                act.wait_ge(c_sum, DC)
                act.activation(con_mu[:, :], stat[:, :], ACT.Copy, scale=1.0 / D).then_inc(c_mu, 1)
                for c in range(DC):
                    act.wait_ge(c_ctr, c + 1)
                    square(con_y[:, c, :])
                act.wait_ge(sq_used, squares.last())
                inverse_rms(D)
                for c in range(DC):
                    n = pre.next()
                    act.wait_ge(y_ready, n)
                    if c >= 2:
                        act.wait_ge(xl_ready, n - 2)
                    act.activation(con_t[:, c % 2, :], y[c % 2][:, :], ACT.Silu, bias=col("conv_ln_b_2", c)).then_inc(c_z, 1)
                    act.wait_ge(c_z, c + 1)
                    act.activation(xh[:, c, :], con_t[:, c % 2, :], ACT.Copy).then_inc(xh_ready, 1)
                residual_out(1, final)
                upd.next()

            hd, hd_in = Tally(), Tally()

            def diff(final):
                norm_x((xh, xqh))
                act.wait_ge(d_lam, 2)
                act.activation(lam_exp, lam_sum, ACT.Exp).then_inc(d_lam, 1)

                def take(dst, ready, value, scale=1.0):
                    split_next()
                    b, t = banks.take()
                    act.activation(dst, lin[b][:, :], ACT.Copy, scale=scale).then_inc(ready, 1)
                    act.wait_ge(ready, value)
                    act.sem_inc(bank_free[b], 1)

                def place_v(p, n):
                    act.wait_ge(d_vr, n)
                    act.activation(dif_v[:, p, :, :], trp[:, :, :], ACT.Copy).then_inc(d_v, 1)

                def exps(n, b):
                    s, w = b % 2, (b + 1) * P
                    act.wait_ge(d_max, (n - 1) * TB + b + 1)
                    act.wait_ge(d_a, (n - 1) * TB + b + 1)
                    for c in range(2):
                        act.activation(dif_e[:, s, c, 0:w], att[:, 2 * s + c, 0:w], ACT.Exp, bias=neg_max[:, s, c:c + 1],
                                       accum_out=den[:, s, c:c + 1]).then_inc(d_e, 1)

                def place_pt(n, b):
                    act.wait_ge(d_tr, (n - 1) * TB + b + 3)
                    act.activation(dif_pt[:, 0:b + 1, b * P:(b + 1) * P], trp[:, 0:b + 1, :], ACT.Copy).then_inc(d_pt, 1)

                def step(p, more):
                    n = hd.next()
                    exps(n, 0)
                    exps(n, 1)
                    if more:
                        take(dif_k[:, 1 - p, :], d_k, n + 1)
                    place_pt(n, 0)
                    place_pt(n, 1)
                    exps(n, 2)
                    exps(n, 3)
                    if more:
                        take(dif_q[:, 1 - p, :], d_q, n + 1, 64 ** -0.5)
                    place_pt(n, 2)
                    place_pt(n, 3)
                    act.wait_ge(d_pv, n)
                    square(att[:, 3, :])
                    act.activation(dif_o[:, :], att[:, 3, :], ACT.Copy).then_inc(d_o, 1)
                    if more:
                        take(dif_vt[:, :], d_vt, n + 1)
                        place_v(1 - p, n + 1)
                    act.wait_ge(sq_used, squares.last())
                    inverse_rms(P)
                    act.wait_ge(d_y, n)
                    act.activation(att_hi[:, bass.ds(n - 1, 1), :] if not isinstance(n, int) else att_hi[:, n - 1, :],
                                   y[0][:, :], ACT.Copy).then_inc(d_hi, 1)

                take(dif_k[:, 0, :], d_k, 1)
                take(dif_q[:, 0, :], d_q, 1, 64 ** -0.5)
                take(dif_vt[:, :], d_vt, 1)
                place_v(0, 1)
                with rounds(act, AH // 2 - 1, (units, 6), (banks, 6), (squares, 2), (rss, 2), (hd, 2)):
                    step(0, True)
                    step(1, True)
                step(0, True)
                step(1, False)
                project_out(dif_hT, 1, final)
                upd.next()

            def ffn(kind, layer, final):
                norm_x()
                cw = {1: "ffn_conv_w", 2: "ffn_w_dw_2"}[kind]
                cb = {1: "ffn_conv_b", 2: "ffn_b_dw_2"}[kind]
                width = 2 * FC if kind == 1 else FC
                with rounds(act, FC, (units, 2), (banks, 2), (f_n, 1)) as i:
                    n = f_n.next()
                    for u in range(kind % 2 + 1 if kind == 1 else 1):
                        split_next()
                        b, t = banks.take()
                        if n_first(n):
                            pass
                        act.activation((ffn_g, ffn_u)[u][:, :], lin[b][:, :], ACT.Identity,
                                       scale=col(cw, i + ((layer * 3 + 2) * width + u * FC)),
                                       bias=col(cb, i + (layer * width + u * FC))).then_inc(f_cu[u], 1)
                    if kind == 2:
                        split_next()
                        banks.take()
                    act.wait_ge(f_cv[0], n)
                    act.activation(ffn_s[:, :], ffn_g[:, :], ACT.Silu).then_inc(f_silu, 1)
                    act.wait_ge(f_prod, n)
                    act.activation(ffn_hi[:, bass.ds(i, 1), :], ffn_p[:, :], ACT.Copy).then_inc(f_hi, 1)
                if kind == 1:
                    project_out(ffn_hT, 3, final)
                    upd.next()
                else:
                    residual_out(3, final)
                    upd.next()

            def n_first(n):
                return False
            f_n = Tally()

            act.dma_start(const[:, :], a["const"]).then_inc(const_in, 16)
            act.dma_start(x_in[:, :, :], a["x"][0].rearrange("(b p) d -> p b d", p=P)).then_inc(x_landed, 16)
            for dst, src in row_dmas(a, rows):
                act.dma_start(dst, src).then_inc(rows_in, 16)
            for s in range(2):
                act.wait_ge(raw_full[s], 16)
                act.activation(w_hi[s][:, :, :], raw[s][:, :, :], ACT.Copy).then_inc(hi_done[s], 1)
            act.wait_ge(tr_done, DC + 1)
            act.activation(params[:, 0:4 * P], trp[:, :, :], ACT.Copy).then_inc(par_done, 1)
            act.wait_ge(tr_done, DC + 2)
            act.activation(params[:, 4 * P:NPARAM], trp[:, :, :].rearrange("p b n -> p (b n)")[:, 0:NPARAM - 4 * P], ACT.Copy).then_inc(par_done, 1)
            act.wait_ge(par_done, 2)
            act.wait_ge(eps_set, 1)
            if run[0]:
                act.dma_start(ret_tab[:, :], a["ret_table"]).then_inc(r_tab, 16)
                retention(last == 0)
            if run[1]:
                ffn(1, 0, last == 1)
            if run[2]:
                act.wait_ge(x_ready, (upd.n + 1) * DC)
                act.dma_start(dif_lp[:, :], a["b_lambda"][0].rearrange("r c -> (r c)").partition_broadcast(P)).then_inc(d_lp, 16)
                diff(last == 2)
            if run[3]:
                ffn(1, 1, last == 3)
            if run[4]:
                conformer(last == 4)
            if run[5]:
                ffn(2, 0, last == 5)
            if run[6]:
                act.wait_ge(x_ready, (upd.n + 1) * DC)
                act.dma_start(n_tabs[:, :], a["nsa_table"]).then_inc(n_tab_in, 16)
                nsa(last == 6)
            if run[7]:
                ffn(2, 1, last == 7)

        @block.vector
        def _(dve):
            units, banks, squares, rss, pre, upd, own, hs, zeros = (
                Turns(), Turns(), Tally(), Tally(), Tally(), Tally(), Tally(), Tally(), Tally())

            def split_next(no_more=False, twice=False):
                s, t = units.take()
                if twice:
                    dve.wait_ge(hi_done[s], t + 2)
                    dve.tensor_tensor(w_lo[s][:, 0:2, :].rearrange("p c (r n) -> p c r n", r=2),
                                      raw[s][:, 0:2, 0:HD].unsqueeze(2).broadcast_to([P, 2, 2, HD]),
                                      w_hi[s][:, 0:2, :].rearrange("p c (r n) -> p c r n", r=2).bitcast(F32), ALU.subtract).then_inc(lo_done[s], 1)
                elif not no_more:
                    dve.wait_ge(hi_done[s], t + 2)
                    dve.tensor_tensor(w_lo[s][:, :, :], raw[s][:, :, :], w_hi[s][:, :, :].bitcast(F32), ALU.subtract).then_inc(lo_done[s], 1)
                return s, t

            def norm_x(gain, g0):
                for c in range(DC):
                    squares.next()
                dve.wait_ge(rs_ready, rss.next())
                scaled(gain, g0)

            def scaled(gain, g0):
                for c in range(DC):
                    n = pre.next()
                    if n > 2:
                        dve.wait_ge(xl_ready, n - 2)
                    dve.scalar_tensor_tensor(y[c % 2][:, :], x[:, c, :], col(gain, g0 + c), rs[:, :], ALU.mult, ALU.mult).then_inc(y_ready, 1)

            def project_out(hT, nu, gain, g0, final=False):
                dve.memset(acc[:, :], 0.0).then_inc(acc_zero, 1)
                zeros.next()

                def one(o, no_more):
                    for n in range(nu):
                        split_next(no_more and o * nu + n >= 2 * nu - 2)
                    v = squares.next()
                    dve.wait_ge(sq_ready, v)
                    dve.wait_ge(sq_used, v - 1)
                    dve.tensor_tensor(acc[:, :], acc[:, :], sq[(squares.n - 1) % 2][:, :], ALU.add).then_inc(sq_used, 1)

                dve.wait_ge(acc_zero, zeros.last())
                n_loop = DC // 2 - (1 if final else 0)
                with rounds(dve, n_loop, (units, 2 * nu), (squares, 2)):
                    for o in range(2):
                        one(o, False)
                if final:
                    for o in range(2):
                        one(o, True)
                for _ in range(DC):
                    banks.take()
                dve.wait_ge(rs_ready, rss.next())
                for c in range(DC):
                    n = upd_t.next()
                    if n > 2:
                        dve.wait_ge(x_ready, upd.n * DC + c - 1 if c >= 2 else upd.n * DC)
                    dve.scalar_tensor_tensor(y[c % 2][:, :], hT[:, c, :], col(gain, g0 + c), rs[:, :], ALU.mult, ALU.mult).then_inc(t_ready, 1)
                upd.next()

            def residual_out(nu, bias=None, final=False):
                def one(o, k, no_more):
                    for n in range(nu):
                        s, t = split_next(no_more and o * nu + n >= 2 * nu - 2)
                    b, _t = banks.take()
                    dve.wait_ge(unit_done[s], t + 1)
                    xc = x[:, k, :] if isinstance(k, int) else x[:, bass.ds(k, 1), :]
                    if bias is None:
                        dve.tensor_tensor(xc, xc, lin[b][:, :], ALU.add).then_inc(x_ready, 1)
                    else:
                        dve.scalar_tensor_tensor(xc, lin[b][:, :], col(bias, k), xc, ALU.add, ALU.add).then_inc(x_ready, 1)
                    xr.next()
                    dve.wait_ge(x_ready, xr.last())
                    dve.sem_inc(bank_free[b], 1)

                xr = Tally()
                xr.base = (upd.n) * DC
                n_loop = DC // 2 - (1 if final else 0)
                with rounds(dve, n_loop, (units, 2 * nu), (banks, 2), (xr, 2)) as i:
                    for o in range(2):
                        one(o, i * 2 + o, False)
                if final:
                    for o in range(2):
                        one(o, DC - 2 + o, True)
                upd.next()

            heads = Tally()
            ret_chain = Tally()

            def retention(final):
                norm_x("a_norm_pre", 0)
                dve.wait_ge(r_tab, 16)
                with rounds(dve, RH, (units, 12), (squares, RC), (rss, 1), (heads, 1), (ret_chain, 8)) as i:
                    h = heads.next()
                    for dst, turn in ((ret_q, 0), (ret_k, 1)):
                        split_next()
                        split_next()
                        dve.wait_ge(r_raw, (h - 1) * 8 + 2 * turn + 2)
                        if turn == 0:
                            pass
                        cos, sin = ret_tab[:, 0:T], ret_tab[:, T:2 * T]
                        for half, (f0, f1, op) in enumerate(((cos, sin, ALU.subtract), (sin, cos, ALU.add))):
                            dve.tensor_tensor(ret_m[:, 0, :], ret_raw[:, 0, :], f0, ALU.mult).then_inc(dve_step, 1)
                            dve.tensor_tensor(ret_m[:, 1, :], ret_raw[:, 1, :], f1, ALU.mult).then_inc(dve_step, 1)
                            ret_chain.next()
                            dve.wait_ge(dve_step, ret_chain.next())
                            done = dve.tensor_tensor(dst[:, half, :], ret_m[:, 0, :], ret_m[:, 1, :], op)
                            if half:
                                done.then_inc(r_rot, 1)
                            else:
                                done.then_inc(r_lo0, 1)
                                dve.wait_ge(r_lo0, (h - 1) * 2 + turn + 1)
                        dve.wait_ge(r_rot, (h - 1) * 2 + turn + 1)
                    for c in range(RC):
                        split_next()
                    split_next()
                    split_next()
                    for j in range(TB):
                        dve.wait_ge(r_s, (h - 1) * TB + j + 1)
                        dve.tensor_tensor(ret_s[j], att[:, j, 0:T - j * P], ret_tab[:, bass.ds(i * T + 2 * T, T - j * P)], ALU.mult).then_inc(r_sd, 1)
                    split_next()
                    split_next()
                    dve.wait_ge(rs_ready, rss.next())
                    for _ in range(RC):
                        squares.next()
                    for c in range(RC):
                        if c >= 2:
                            dve.wait_ge(r_lo, (h - 1) * RC + c - 1)
                        dve.tensor_tensor(y[c % 2][:, :], ret_o[:, c, :], rs[:, :], ALU.mult).then_inc(r_p, 1)
                        dve.wait_ge(r_p, (h - 1) * 2 * RC + 2 * c + 1)
                        dve.tensor_tensor(y[c % 2][:, :], y[c % 2][:, :], ret_g[:, c, :], ALU.mult).then_inc(r_p, 1)
                        if c:
                            low(i, h, c - 1)
                    low(i, h, RC - 1)
                project_out(ret_hT, 2, "a_norm_post", 0, final)

            def low(i, h, c):
                dve.wait_ge(r_hi, (h - 1) * RC + c + 1)
                dve.tensor_tensor(ret_lo[:, bass.ds(i * RC + c, 1), :], y[c % 2][:, :], ret_hi[:, bass.ds(i * RC + c, 1), :].bitcast(F32), ALU.subtract).then_inc(r_lo, 1)

            ropes, steps = Tally(), Tally()

            def nsa(final):
                norm_x("mix_norm_g_2", DC)
                dve.wait_ge(n_tab_in, 16)
                NC = NG * NCMP
                cos, sin = n_tabs[:, 0:T], n_tabs[:, T:2 * T]
                for n, pe_ in enumerate(("nsa_pe_k_2", "nsa_pe_v_2")):
                    for pair in range(2):
                        s, t = split_next()
                        b, _t = banks.take()
                        dve.wait_ge(unit_done[s], t + 1)
                        if n and pair == 0:
                            dve.wait_ge(n_zl, 1)
                        for g2 in range(2):
                            tokens = lin[b][g2 * HD:(g2 + 1) * HD, :].rearrange("p (m l o) -> p o l m", l=8, o=2)
                            for l2 in range(2):
                                for h8 in range(2):
                                    r = slice(l2 * HD, (l2 + 1) * HD)
                                    at = PARAM_AT[pe_] + 8 * h8
                                    dve.tensor_tensor(z[r, 8 * h8:8 * h8 + 8, 2 * pair + g2, :], tokens[:, l2, :, h8:h8 + NCMP],
                                                      params[r, at:at + 8].unsqueeze(2).broadcast_to([HD, 8, NCMP]), ALU.add).then_inc(n_z, 1)
                        dve.wait_ge(n_z, 16 * n + 8 * (pair + 1))
                        dve.sem_inc(bank_free[b], 1)
                    dve.wait_ge(n_zh, n + 1)
                    dve.tensor_tensor(z_lo[n][:, :, :], z[:, :, :, :].rearrange("p l g n -> p l (g n)"), z_hi[n][:, :, :].bitcast(F32),
                                      ALU.subtract).then_inc(n_zl, 1)

                def rotate(b, src, n, outs):
                    dve.wait_ge(n_sw, n)
                    dve.tensor_tensor(n_t[:, 0, :], src, cos, ALU.mult).then_inc(n_tt, 1)
                    dve.tensor_tensor(n_t[:, 1, :], lin[b][:, :], sin, ALU.mult).then_inc(n_tt, 1)
                    dve.wait_ge(n_tt, 2 * n)
                    dve.sem_inc(bank_free[b], 1)
                    outs()

                with rounds(dve, 2, (units, 2), (banks, 2), (rss, 2), (ropes, 2), (squares, 2)) as i:
                    bs = []
                    for c in range(2):
                        split_next()
                        bs.append(banks.take()[0])
                        squares.next()
                    for c in range(2):
                        n = ropes.next()
                        dve.wait_ge(rs_ready, rss.next())
                        if c:
                            dve.wait_ge(n_sw, n - 1)
                        dve.scalar_tensor_tensor(y[0][:, :], n_raw[:, c, :], col("nsa_ks_norm_2", i), rs[:, :], ALU.mult, ALU.mult).then_inc(n_yn, 1)
                        dve.wait_ge(n_yn, n)

                        def outs():
                            for half in range(2):
                                r = slice(half * HD, half * HD + HD)
                                dve.tensor_tensor(k_all[r, bass.ds(i, 1), 2 * c + half, :], n_t[r, 0:1, :], n_t[r, 1:2, :], ALU.add).then_inc(n_kr, 1)
                            dve.wait_ge(n_kr, 2 * n)
                        rotate(bs[c], y[0][:, :], n, outs)
                with rounds(dve, 2, (units, 2), (banks, 2)):
                    for _ in range(2):
                        split_next()
                        banks.take()
                split_next()
                banks.take()
                for n in range(2):
                    for m_ in range(HID // P):
                        w2_next = n == 1 and m_ == 1
                        split_next(twice=w2_next)
                        split_next(twice=w2_next)
                        banks.take()
                        dve.wait_ge(n_hh, 2 * n + m_ + 1)
                        dve.tensor_tensor(hid_of[n][1][:, m_, :], hid[:, m_, :], hid_of[n][0][:, m_, :].bitcast(F32), ALU.subtract).then_inc(n_hl, 1)
                split_next()
                banks.take()
                squares.next()
                dve.wait_ge(rs_ready, rss.next())
                dve.scalar_tensor_tensor(kc_all[:, :], n_raw[:, 0, 0:NC], col("nsa_kc_norm_2"), rs[:, 0:NC], ALU.mult, ALU.mult).then_inc(n_kc, 1)
                split_next()
                banks.take()
                dve.tensor_scalar(q_gain[:, 0:1], col("nsa_q_norm_2"), HD ** -0.5, None, ALU.mult).then_inc(q_g, 1)
                dve.wait_ge(q_g, 1)
                dve.wait_ge(n_vcd, 1)

                def stage(g):
                    ds = (lambda at, k: slice(at, at + k)) if isinstance(g, int) else bass.ds
                    dve.tensor_copy(vst[:, :, :, :], v_all[:, :, :, ds(g * HD, HD)]).then_inc(n_vst, 1)
                    dve.tensor_copy(vcst[0:NCMP, :].unsqueeze(1), vc_all[0:NCMP, ds(g, 1), :]).then_inc(n_vst, 1)

                def normed_q(p):
                    squares.next()
                    dve.wait_ge(rs_ready, rss.next())
                    n = ropes.next()
                    dve.scalar_tensor_tensor(qn[:, p, :], n_raw[:, p, :], q_gain[:, 0:1], rs[:, :], ALU.mult, ALU.mult).then_inc(n_yn, 1)
                    dve.wait_ge(n_yn, n)
                    return n

                def rotated_q(p, b, n):
                    def outs():
                        dve.tensor_tensor(qr[:, p, :], n_t[:, 0, :], n_t[:, 1, :], ALU.add).then_inc(n_qr, 1)
                        dve.wait_ge(n_qr, n - 4)
                    rotate(b, qn[:, p, :], n, outs)

                def top(n, it):
                    blk, sl = it % TB, it % 2
                    dve.wait_ge(n_s, (n - 1) * 8 + it + 1)
                    diag = att[:, 2 * sl:2 * sl + 2, blk * P:(blk + 1) * P]
                    dve.tensor_tensor(diag, diag, c_("causal").unsqueeze(1).broadcast_to([P, 2, P]), ALU.add).then_inc(n_mask, 1)
                    dve.wait_ge(n_mask, (n - 1) * 8 + it + 1)
                    dve.tensor_reduce(n_max[:, sl, :], att[:, 2 * sl:2 * sl + 2, 0:(blk + 1) * P], AX_X, ALU.max, negate=True).then_inc(n_mx, 1)

                def weights(n, it, j):
                    hh, blk, sl, w = it // TB, it % TB, it % 2, (it % TB + 1) * P
                    at = ((n - 1) * 8 + it) * 3
                    dve.wait_ge(n_ex, (n - 1) * 16 + 2 * it + 2)
                    dve.reciprocal(n_inv[:, sl, :], n_den[:, sl, :]).then_inc(n_w, 1)
                    dve.wait_ge(n_w, at + 1)
                    k = 6 * j + (3 * hh + 1)
                    gate = gates[:, blk, k:k + 2] if isinstance(j, int) else gates[:, blk, bass.ds(k, 2)]
                    dve.tensor_tensor(n_inv[:, sl, :], n_inv[:, sl, :], gate, ALU.mult).then_inc(n_w, 1)
                    dve.wait_ge(n_w, at + 2)
                    dve.tensor_scalar(n_e[:, sl, 0, 0:w], n_e[:, sl, 0, 0:w], n_inv[:, sl, 0:1], None, ALU.mult).then_inc(n_w, 1)
                    dve.tensor_scalar(n_e[:, sl, 1, 0:w], n_e[:, sl, 1, 0:w], n_inv[:, sl, 1:2], None, ALU.mult).then_inc(n_a, 1)
                    dve.wait_ge(n_w, at + 3)

                seen = n_tabs[:, 2 * T:2 * T + TB * NP32].rearrange("p (b n) -> p b n", b=TB)[:, :, 0:NCMP]
                unseen = n_tabs[:, 2 * T + TB * NP32:].rearrange("p (b n) -> p b n", b=TB)[:, :, 0:NCMP]

                def compressed_top(n, bo):
                    dve.wait_ge(n_cs, n)
                    for hh, src in enumerate((lin[bo], stat)):
                        dve.tensor_tensor(ce[:, hh * TB:(hh + 1) * TB, 0:NCMP], src[:, 0:TB * NP32].rearrange("p (b n) -> p b n", b=TB)[:, :, 0:NCMP],
                                          unseen, ALU.add).then_inc(n_c, 1)
                    dve.wait_ge(n_c, (n - 1) * 10 + 2)
                    dve.tensor_reduce(c_max, ce[:, :, 0:NCMP], AX_X, ALU.max).then_inc(n_c, 1)
                    dve.wait_ge(n_c, (n - 1) * 10 + 3)
                    dve.tensor_tensor(ce[:, :, 0:NCMP], ce[:, :, 0:NCMP], c_max.unsqueeze(2).broadcast_to([P, 8, NCMP]), ALU.subtract).then_inc(n_c, 1)

                def compressed_weights(n, j):
                    at = (n - 1) * 10
                    dve.wait_ge(n_ce, n)
                    v = ce[:, :, :].rearrange("p (h b) n -> p h b n", h=2)[:, :, :, 0:NCMP]
                    dve.tensor_tensor(v, v, seen.unsqueeze(1).broadcast_to([P, 2, TB, NCMP]), ALU.mult).then_inc(n_c, 1)
                    dve.wait_ge(n_c, at + 5)
                    dve.tensor_reduce(c_den, ce[:, :, 0:NCMP], AX_X, ALU.add).then_inc(n_c, 1)
                    dve.wait_ge(n_c, at + 6)
                    dve.tensor_scalar(c_den, c_den, 1e-30, None, ALU.max).then_inc(n_c, 1)
                    dve.wait_ge(n_c, at + 7)
                    dve.reciprocal(c_den, c_den).then_inc(n_c, 1)
                    dve.wait_ge(n_c, at + 8)
                    gate = gates[:, :, 6 * j:6 * j + 6] if isinstance(j, int) else gates[:, :, bass.ds(6 * j, 6)]
                    d_ = c_den.rearrange("p (h b) -> p h b", h=2)
                    dve.tensor_tensor(d_, d_, gate.rearrange("p b (h r) -> p h b r", h=2)[:, :, :, 0], ALU.mult).then_inc(n_c, 1)
                    dve.wait_ge(n_c, at + 9)
                    dve.tensor_tensor(ce[:, :, 0:NCMP], ce[:, :, 0:NCMP], c_den.unsqueeze(2).broadcast_to([P, 8, NCMP]), ALU.mult).then_inc(n_c, 1)

                def step(p, more):
                    n = steps.next()
                    j = n - 1
                    bo, bt = banks.take()
                    compressed_top(n, bo)
                    top(n, 0)
                    top(n, 1)
                    compressed_weights(n, j)
                    weights(n, 0, j)
                    weights(n, 1, j)
                    if more:
                        split_next()
                        b, _t = banks.take()
                    for it in (2, 3):
                        top(n, it)
                    if more:
                        r = normed_q(1 - p)
                    weights(n, 2, j)
                    top(n, 4)
                    weights(n, 3, j)
                    top(n, 5)
                    if more:
                        rotated_q(1 - p, b, r)
                    for it in (4, 5):
                        weights(n, it, j)
                        top(n, it + 2)
                    weights(n, 6, j)
                    weights(n, 7, j)
                    dve.wait_ge(n_o, n)
                    k = slice(j, j + 1) if isinstance(j, int) else bass.ds(j, 1)
                    dve.tensor_tensor(att_lo[:, k, :], lin[bo][:, :].unsqueeze(1), att_hi[:, k, :].bitcast(F32), ALU.subtract).then_inc(n_lo, 1)
                    dve.wait_ge(n_lo, n)
                    dve.sem_inc(bank_free[bo], 1)

                split_next()
                b, _t = banks.take()
                r = normed_q(0)
                rotated_q(0, b, r)
                with rounds(dve, NG - 1, (units, 2), (banks, 4), (squares, 2), (rss, 2), (ropes, 2), (steps, 2)) as g:
                    stage(g)
                    step(0, True)
                    step(1, True)
                stage(NG - 1)
                step(0, True)
                step(1, False)
                residual_out(1, None, final)

            def conformer(final):
                norm_x("mix_norm_g_2", 0)
                dve.memset(con_u[:, 0:CW - 1], 0.0).then_inc(c_pad, 1)
                dve.wait_ge(c_pad, 1)
                cn = Tally()
                own_taps = CW - POOL_TAPS
                with rounds(dve, DC, (units, 2), (banks, 2), (cn, 1)) as i:
                    n = cn.next()
                    split_next()
                    banks.take()
                    s, t = split_next()
                    b, _t = banks.take()
                    dve.wait_ge(unit_done[s], t + 1)
                    dve.wait_ge(c_sig, n)
                    dve.scalar_tensor_tensor(con_u[:, CW - 1:], lin[b][:, :], col("conv_b_pw1_2", i), con_s[:, :], ALU.add, ALU.mult).then_inc(c_u, 1)
                    dve.wait_ge(c_u, n)
                    dve.sem_inc(bank_free[b], 1)
                    at = (n - 1) * (own_taps + 1)
                    for j in range(own_taps):
                        part = con_a[:, j % 2, :]
                        if j >= 2:
                            dve.wait_ge(c_own, at + j - 1)
                        if j == 0:
                            done = dve.tensor_scalar(part, con_u[:, 0:T], col("conv_w_dw_2", i), col("conv_b_dw_2", i), ALU.mult, ALU.add)
                        elif j == 1:
                            done = dve.tensor_scalar(part, con_u[:, 1:1 + T], col("conv_w_dw_2", i + DC), None, ALU.mult)
                        else:
                            done = dve.scalar_tensor_tensor(part, con_u[:, j:j + T], col("conv_w_dw_2", i + j * DC), part, ALU.mult, ALU.add)
                        done.then_inc(c_own, 1)
                    dve.wait_ge(c_own, at + own_taps)
                    dve.tensor_tensor(con_a[:, 0, :], con_a[:, 0, :], con_a[:, 1, :], ALU.add).then_inc(c_own, 1)
                    dve.wait_ge(c_own, at + own_taps + 1)
                    dve.wait_ge(c_add, (n - 1) * (POOL_TAPS - 1) + POOL_TAPS - 1)
                    dve.tensor_tensor(con_y[:, bass.ds(i, 1), :], con_a[:, 0:1, :], con_a[:, 2:3, :], ALU.add).then_inc(c_y, 1)
                    dve.wait_ge(c_y, n)
                dve.wait_ge(c_mu, 1)
                for c in range(DC):
                    dve.tensor_tensor(con_y[:, c, :], con_y[:, c, :], con_mu[:, :], ALU.subtract).then_inc(c_ctr, 1)
                for c in range(DC):
                    squares.next()
                dve.wait_ge(rs_ready, rss.next())
                for c in range(DC):
                    n = pre.next()
                    dve.wait_ge(xl_ready, n - 2)
                    dve.scalar_tensor_tensor(y[c % 2][:, :], con_y[:, c, :], col("conv_ln_g_2", c), rs[:, :], ALU.mult, ALU.mult).then_inc(y_ready, 1)
                residual_out(1, "conv_b_pw2_2", final)

            hd = Tally()

            def diff(final):
                dve.wait_ge(d_lp, 16)
                lp = dif_lp[:, :].rearrange("p (m o c) -> p m o c", m=2, o=2)
                dve.tensor_tensor(dif_lq[:, :, :], lp[:, :, 0, :], lp[:, :, 1, :], ALU.mult).then_inc(d_lam, 1)
                dve.wait_ge(d_lam, 1)
                dve.tensor_reduce(lam_sum, dif_lq[:, :, :], AX_X, ALU.add).then_inc(d_lam, 1)
                norm_x("kv_norm", 0)
                scaled("b_norm_pre", 0)
                dve.wait_ge(d_lam, 3)
                dve.scalar_tensor_tensor(neg_lam, lam_exp[:, 1:2], -LAMBDA_INIT, lam_exp[:, 0:1], ALU.add, ALU.subtract).then_inc(d_lam, 1)
                dve.tensor_scalar(sub_g, col("b_subln"), 1.0 - LAMBDA_INIT, None, ALU.mult).then_inc(d_lam, 1)
                dve.wait_ge(d_lam, 5)

                def top(n, b):
                    s, w = b % 2, (b + 1) * P
                    dve.wait_ge(d_s, (n - 1) * TB + b + 1)
                    diag = att[:, 2 * s:2 * s + 2, b * P:(b + 1) * P]
                    dve.tensor_tensor(diag, diag, c_("causal").unsqueeze(1).broadcast_to([P, 2, P]), ALU.add).then_inc(d_mask, 1)
                    dve.wait_ge(d_mask, (n - 1) * TB + b + 1)
                    dve.tensor_reduce(neg_max[:, s, :], att[:, 2 * s:2 * s + 2, 0:w], AX_X, ALU.max, negate=True).then_inc(d_max, 1)

                def difference(n, b):
                    s, w = b % 2, (b + 1) * P
                    dve.wait_ge(d_e, (n - 1) * 2 * TB + 2 * b + 2)
                    at = ((n - 1) * TB + b) * 3
                    dve.reciprocal(inv_den[:, s, :], den[:, s, :]).then_inc(d_w, 1)
                    dve.wait_ge(d_w, at + 1)
                    dve.tensor_tensor(inv_den[:, s, 1:2], inv_den[:, s, 1:2], neg_lam, ALU.mult).then_inc(d_w, 1)
                    dve.wait_ge(d_tr, (n - 1) * TB + b + 1)
                    dve.tensor_scalar(dif_a[:, s, 0:w], dif_e[:, s, 0, 0:w], inv_den[:, s, 0:1], None, ALU.mult).then_inc(d_w, 1)
                    dve.wait_ge(d_w, at + 3)
                    dve.scalar_tensor_tensor(dif_a[:, s, 0:w], dif_e[:, s, 1, 0:w], inv_den[:, s, 1:2], dif_a[:, s, 0:w],
                                             ALU.mult, ALU.add).then_inc(d_a, 1)

                def step(more):
                    n = hd.next()
                    top(n, 0)
                    top(n, 1)
                    difference(n, 0)
                    difference(n, 1)
                    if more:
                        split_next()
                    top(n, 2)
                    top(n, 3)
                    difference(n, 2)
                    difference(n, 3)
                    if more:
                        split_next()
                        split_next()
                    squares.next()
                    dve.wait_ge(rs_ready, rss.next())
                    dve.scalar_tensor_tensor(y[0][:, :], dif_o[:, :], sub_g, rs[:, :], ALU.mult, ALU.mult).then_inc(d_y, 1)
                    dve.wait_ge(d_hi, n)
                    k = bass.ds(n - 1, 1) if not isinstance(n, int) else slice(n - 1, n)
                    dve.tensor_tensor(att_lo[:, k, :], y[0][:, :].unsqueeze(1), att_hi[:, k, :].bitcast(F32), ALU.subtract).then_inc(d_lo, 1)
                    dve.wait_ge(d_lo, n)

                for _ in range(3):
                    split_next()
                with rounds(dve, AH // 2 - 1, (units, 6), (squares, 2), (rss, 2), (hd, 2)):
                    step(True)
                    step(True)
                step(True)
                step(False)
                project_out(dif_hT, 1, "b_norm_post", 0, final)

            f_n, f_w = Tally(), Tally()

            def ffn(kind, layer, final):
                gain = {1: "ffn_norm_pre", 2: "ffn_norm_g_2"}[kind]
                norm_x(gain, layer * DC)
                cw = {1: "ffn_conv_w", 2: "ffn_w_dw_2"}[kind]
                width = 2 * FC if kind == 1 else FC
                with rounds(dve, FC, (units, 2), (banks, 2), (f_n, 1)) as i:
                    n = f_n.next()
                    bs = []
                    for u in range(2 if kind == 1 else 1):
                        split_next()
                        b, t = banks.take()
                        tile = (ffn_g, ffn_u)[u]
                        dve.wait_ge(f_cu[u], n)
                        dve.scalar_tensor_tensor(tile[:, 1:T], lin[b][:, 0:T - 1], col(cw, i + ((layer * 3 + 1) * width + u * FC)),
                                                 tile[:, 1:T], ALU.mult, ALU.add).then_inc(f_tap[u], 1)
                        dve.wait_ge(f_tap[u], n if u == 0 else i + (n_u[0] + 1))
                        dve.scalar_tensor_tensor(tile[:, 2:T], lin[b][:, 0:T - 2], col(cw, i + ((layer * 3) * width + u * FC)),
                                                 tile[:, 2:T], ALU.mult, ALU.add).then_inc(f_cv[u], 1)
                        dve.wait_ge(f_cv[u], n if u == 0 else i + (n_u[0] + 1))
                        dve.sem_inc(bank_free[b], 1)
                    if kind == 2:
                        s, t = split_next()
                        b, _t = banks.take()
                        dve.wait_ge(unit_done[s], t + 1)
                    dve.wait_ge(f_silu, n)
                    if kind == 1:
                        dve.tensor_tensor(ffn_p[:, :], ffn_s[:, :], ffn_u[:, :], ALU.mult).then_inc(f_prod, 1)
                    else:
                        dve.tensor_tensor(ffn_p[:, :], ffn_s[:, :], lin[b][:, :], ALU.mult).then_inc(f_prod, 1)
                        dve.wait_ge(f_prod, n)
                        dve.sem_inc(bank_free[b], 1)
                    dve.wait_ge(f_hi, n)
                    dve.tensor_tensor(ffn_lo[:, bass.ds(i, 1), :], ffn_p[:, :], ffn_hi[:, bass.ds(i, 1), :].bitcast(F32), ALU.subtract).then_inc(f_lo, 1)
                    dve.wait_ge(f_lo, n)
                if kind == 1:
                    n_u[0] += FC
                    project_out(ffn_hT, 3, "ffn_norm_post", layer * DC, final)
                else:
                    residual_out(3, None, final)

            n_u = [0]
            upd_t = Tally()

            for s in range(2):
                dve.sem_inc(lo_done[s], 1)
                dve.sem_inc(bank_free[s], 1)
            dve.sem_inc(r_v, 1)
            dve.sem_inc(d_o, 1)
            dve.sem_inc(d_a, 2)
            dve.sem_inc(d_tr, 2)
            dve.sem_inc(n_tr, 4)
            for c in range(DC):
                dve.wait_ge(tr_done, c + 1)
                dve.tensor_copy(x[:, c, :], att[:, c % 4, :]).then_inc(x_ready, 1)
            upd.next()
            for s in range(2):
                dve.wait_ge(hi_done[s], 1)
                dve.tensor_tensor(w_lo[s][:, :, :], raw[s][:, :, :], w_hi[s][:, :, :].bitcast(F32), ALU.subtract).then_inc(lo_done[s], 1)
            dve.wait_ge(par_done, 2)
            if run[0]:
                retention(last == 0)
            if run[1]:
                ffn(1, 0, last == 1)
            if run[2]:
                diff(last == 2)
            if run[3]:
                ffn(1, 1, last == 3)
            if run[4]:
                conformer(last == 4)
            if run[5]:
                ffn(2, 0, last == 5)
            if run[6]:
                nsa(last == 6)
            if run[7]:
                ffn(2, 1, last == 7)
            for b in range(TB):
                for half in range(2):
                    n = 2 * b + half
                    dve.wait_ge(tr_done, DC + 2 + n + 1)
                    dve.tensor_copy(x_out[:, b, half * T:(half + 1) * T], att[:, n % 4, :]).then_inc(xo_done, 1)


_OUTS = [((1, T, D), "float32")]
_ARGS = (
    "x a_norm_pre a_norm_post a_w_in a_w_out kv_norm w_kv b_norm_pre b_norm_post b_w_q b_lambda b_subln b_w_out "
    "ffn_norm_pre ffn_norm_post ffn_w_up ffn_conv_w ffn_conv_b ffn_w_down mix_norm_g_2 ffn_norm_g_2 conv_w_pw1_2 "
    "conv_b_pw1_2 conv_w_dw_2 conv_b_dw_2 conv_ln_g_2 conv_ln_b_2 conv_w_pw2_2 conv_b_pw2_2 nsa_w_in_2 nsa_q_norm_2 "
    "nsa_kc_norm_2 nsa_ks_norm_2 nsa_kw_norm_2 nsa_pe_k_2 nsa_pe_v_2 nsa_ck_w1_2 nsa_ck_w2_2 nsa_cv_w1_2 "
    "nsa_cv_w2_2 nsa_w_out_2 ffn_w_up_2 ffn_w_dw_2 ffn_b_dw_2 ffn_w_down_2").split()


def kernel(**inputs):
    import concourse.bacc as bacc
    from concourse.bass_utils import run_bass_kernel_spmd

    nc = bacc.Bacc("TRN2", target_bir_lowering=False, num_devices=1)
    arrays = {name: np.ascontiguousarray(inputs[name]) for name in _ARGS}
    arrays["const"], arrays["ret_table"], arrays["nsa_table"] = tables()
    a = {name: nc.dram_tensor(f"in_{name}", v.shape, mybir.dt.from_np(v.dtype), kind="ExternalInput").ap()
         for name, v in arrays.items()}
    out = nc.dram_tensor("out", _OUTS[0][0], F32, kind="ExternalOutput").ap()
    program(nc, a, out)
    r = run_bass_kernel_spmd(nc, [{f"in_{name}": v for name, v in arrays.items()}], core_ids=[0])
    return r.results[0]["out"]
```
